# Optimizing a Trainium2 kernel written in Bass

```python
import math
import jax, jax.numpy as jnp
from jax import lax
import numpy as np

D_MODEL = 1024
BATCH = 1
SEQ = 512
DEPTH = 2

CHUNK = 64
N_META = 16
N_A_LAYERS = DEPTH // 2
N_B_LAYERS = DEPTH - N_A_LAYERS
DN_ALPHA = (2.0 * DEPTH) ** 0.25
DN_BETA = (8.0 * DEPTH) ** -0.25
LN_EPS = 1e-5
RMS_EPS = 1e-6

SSM_D_INNER = 2 * D_MODEL
SSM_HEAD_DIM = 64
SSM_HEADS = SSM_D_INNER // SSM_HEAD_DIM
SSM_GROUPS = 4
SSM_STATE = 128
SSM_CONV = 4
SSM_CONV_DIM = SSM_D_INNER + 2 * SSM_GROUPS * SSM_STATE
SSM_IN_DIM = SSM_D_INNER + SSM_CONV_DIM + SSM_HEADS
SSM_PAD = (-N_META) % CHUNK

MLA_HEADS = 16
Q_LORA = 384
KV_LORA = 256
QK_NOPE = 64
QK_ROPE = 32
V_HEAD = 64
ROPE_THETA = 10000.0
Q_BLOCK = 128
ATT_PAD = (-N_META) % Q_BLOCK

D_FF = 2816
FFN_CONV = 3

kernel_name = "yoco_mamba2_mla_convffn_deepnorm"

def layer_norm(x, g, b):
    xf = x.astype(jnp.float32)
    mu = jnp.mean(xf, axis=-1, keepdims=True)
    var = jnp.mean(jnp.square(xf - mu), axis=-1, keepdims=True)
    return ((xf - mu) * lax.rsqrt(var + LN_EPS) * g + b).astype(x.dtype)

def rms_norm(x, g):
    xf = x.astype(jnp.float32)
    y = xf * lax.rsqrt(jnp.mean(jnp.square(xf), axis=-1, keepdims=True) + RMS_EPS)
    return y.astype(x.dtype) * g

def causal_dwconv(x, w, b):
    k = w.shape[0]
    y = lax.conv_general_dilated(x, w[:, None, :].astype(x.dtype), window_strides=(1,),
                                 padding=[(k - 1, 0)],
                                 dimension_numbers=("NWC", "WIO", "NWC"),
                                 feature_group_count=x.shape[-1])
    return y + b

def rope_tables(length):
    half = QK_ROPE // 2
    pos = jnp.arange(length, dtype=jnp.float32)
    inv_freq = ROPE_THETA ** (-jnp.arange(half, dtype=jnp.float32) * 2.0 / QK_ROPE)
    ang = pos[:, None] * inv_freq[None, :]
    return jnp.cos(ang), jnp.sin(ang)

def rope(x, cos, sin):
    half = QK_ROPE // 2
    x1, x2 = x[..., :half], x[..., half:]
    return jnp.concatenate([x1 * cos - x2 * sin, x2 * cos + x1 * sin], axis=-1)

def ssd_scan(x, dA, bm, cm):
    b, t, h, p = x.shape
    g, n = bm.shape[2], bm.shape[3]
    r = h // g
    c = t // CHUNK
    xc = x.reshape(b, c, CHUNK, g, r, p)
    bc = bm.reshape(b, c, CHUNK, g, n)
    cc = cm.reshape(b, c, CHUNK, g, n)
    a = dA.astype(jnp.float32).reshape(b, c, CHUNK, g, r).transpose(0, 3, 4, 1, 2)
    a_cs = jnp.cumsum(a, axis=-1)
    tri = jnp.tril(jnp.ones((CHUNK, CHUNK), dtype=bool))
    seg = a_cs[..., :, None] - a_cs[..., None, :]
    decay_in = jnp.where(tri, jnp.exp(jnp.where(tri, seg, 0.0)), 0.0)
    cb = jnp.einsum("bclgn,bcsgn->bgcls", cc, bc)
    y_diag = jnp.einsum("bgrcls,bcsgrp->bclgrp", cb[:, :, None] * decay_in, xc)
    decay_states = jnp.exp(a_cs[..., -1:] - a_cs)
    states = jnp.einsum("bcsgn,bgrcs,bcsgrp->cbgrpn", bc, decay_states, xc)
    chunk_decay = jnp.exp(a_cs[..., -1]).transpose(3, 0, 1, 2)

    def step(state, inp):
        st, dc = inp
        return state * dc[..., None, None] + st, state

    h0 = jnp.zeros((b, g, r, p, n), dtype=states.dtype)
    _, prev = lax.scan(step, h0, (states, chunk_decay))
    y_off = jnp.einsum("bclgn,cbgrpn,bgrcl->bclgrp", cc, prev, jnp.exp(a_cs))
    return (y_diag + y_off).reshape(b, t, h, p)

def mamba2_mixer(u, w_in, conv_w, conv_b, dt_bias, a_log, d_skip, norm_g, w_out):
    bsz, length, _ = u.shape
    zxbcdt = u @ w_in
    z, xbc, dt = jnp.split(zxbcdt, [SSM_D_INNER, SSM_D_INNER + SSM_CONV_DIM], axis=-1)
    xbc = jax.nn.silu(causal_dwconv(xbc, conv_w, conv_b))
    xs, bm, cm = jnp.split(xbc, [SSM_D_INNER, SSM_D_INNER + SSM_GROUPS * SSM_STATE], axis=-1)
    xs = xs.reshape(bsz, length, SSM_HEADS, SSM_HEAD_DIM)
    bm = bm.reshape(bsz, length, SSM_GROUPS, SSM_STATE)
    cm = cm.reshape(bsz, length, SSM_GROUPS, SSM_STATE)
    dt = jax.nn.softplus((dt + dt_bias).astype(jnp.float32))
    dA = dt * (-jnp.exp(a_log.astype(jnp.float32)))

    def pad(t):
        return jnp.pad(t, [(0, 0), (SSM_PAD, 0)] + [(0, 0)] * (t.ndim - 2))

    y = ssd_scan(pad(xs * dt[..., None]), pad(dA), pad(bm), pad(cm))[:, SSM_PAD:]
    y = (y + xs * d_skip[:, None]).reshape(bsz, length, SSM_D_INNER)
    yg = (y * jax.nn.silu(z)).reshape(bsz, length, SSM_GROUPS, SSM_D_INNER // SSM_GROUPS)
    ygf = yg.astype(jnp.float32)
    ygf = ygf * lax.rsqrt(jnp.mean(jnp.square(ygf), axis=-1, keepdims=True) + RMS_EPS)
    yn = ygf.reshape(bsz, length, SSM_D_INNER).astype(u.dtype) * norm_g
    return yn @ w_out

def conv_ffn(u, w_in, conv_w, conv_b, w_out):
    hid = causal_dwconv(u @ w_in, conv_w, conv_b)
    gate, up = jnp.split(hid, [D_FF], axis=-1)
    return (jax.nn.silu(gate) * up) @ w_out

def mla_shared_kv(hs, w_down, norm_g, w_up, cos, sin):
    bsz, length, _ = hs.shape
    kv_a = hs @ w_down
    c_kv = rms_norm(kv_a[..., :KV_LORA], norm_g)
    k_pe = rope(kv_a[..., KV_LORA:], cos, sin)
    kv = (c_kv @ w_up).reshape(bsz, length, MLA_HEADS, QK_NOPE + V_HEAD)
    k_nope, v = kv[..., :QK_NOPE], kv[..., QK_NOPE:]
    padt = lambda t: jnp.pad(t, [(0, 0), (ATT_PAD, 0)] + [(0, 0)] * (t.ndim - 2))
    return padt(k_nope), padt(k_pe), padt(v)

def mla_attention(hs, w_dq, q_norm_g, w_uq, w_o, k_nope, k_pe, v, cos, sin):
    bsz, length, _ = hs.shape
    c_q = rms_norm(hs @ w_dq, q_norm_g)
    q = (c_q @ w_uq).reshape(bsz, length, MLA_HEADS, QK_NOPE + QK_ROPE)
    q_nope = q[..., :QK_NOPE]
    q_pe = rope(q[..., QK_NOPE:], cos[:, None], sin[:, None])
    lp = length + ATT_PAD
    nb = lp // Q_BLOCK

    def to_blocks(t):
        t = jnp.pad(t, ((0, 0), (ATT_PAD, 0), (0, 0), (0, 0)))
        return t.reshape(bsz, nb, Q_BLOCK, MLA_HEADS, t.shape[-1]).swapaxes(0, 1)

    k_pos = jnp.arange(lp)
    k_chunk = k_pos // CHUNK
    k_valid = k_pos >= ATT_PAD
    scale = (QK_NOPE + QK_ROPE) ** -0.5

    def attend_block(args):
        qn, qp, blk = args
        s = (jnp.einsum("bqhd,bkhd->bhqk", qn, k_nope)
             + jnp.einsum("bqhd,bkd->bhqk", qp, k_pe)).astype(jnp.float32) * scale
        q_chunk = (blk * Q_BLOCK + jnp.arange(Q_BLOCK)) // CHUNK
        mask = (k_chunk[None, :] <= q_chunk[:, None]) & k_valid[None, :]
        prob = jax.nn.softmax(jnp.where(mask, s, -1e30), axis=-1)
        return jnp.einsum("bhqk,bkhd->bqhd", prob.astype(v.dtype), v)

    o = lax.map(attend_block, (to_blocks(q_nope), to_blocks(q_pe), jnp.arange(nb)))
    o = o.swapaxes(0, 1).reshape(bsz, lp, MLA_HEADS * V_HEAD)[:, ATT_PAD:]
    return o @ w_o

def setup_inputs(seed: int = 0) -> dict:
    key = jax.random.key(seed)
    ks = iter(jax.random.split(key, 32))
    f32 = jnp.float32

    def dense(shape, fan_in, scale=1.0):
        return jax.random.normal(next(ks), shape, f32) * (fan_in ** -0.5) * scale

    def near_one(shape):
        return 1.0 + 0.02 * jax.random.normal(next(ks), shape, f32)

    def small(shape, s=0.01):
        return s * jax.random.normal(next(ks), shape, f32)

    na, nbl = N_A_LAYERS, N_B_LAYERS
    x = jax.random.normal(next(ks), (BATCH, SEQ, D_MODEL), f32)
    meta_tokens = jax.random.normal(next(ks), (N_META, D_MODEL), f32)
    m_w_in = dense((na, D_MODEL, SSM_IN_DIM), D_MODEL)
    m_conv_w = dense((na, SSM_CONV, SSM_CONV_DIM), SSM_CONV)
    m_conv_b = small((na, SSM_CONV_DIM))
    dt0 = jnp.exp(jax.random.uniform(next(ks), (na, SSM_HEADS), f32,
                                     math.log(1e-3), math.log(1e-1)))
    m_dt_bias = dt0 + jnp.log(-jnp.expm1(-dt0))
    m_a_log = jnp.log(jax.random.uniform(next(ks), (na, SSM_HEADS), f32, 1.0, 16.0))
    m_d = 1.0 + 0.1 * jax.random.normal(next(ks), (na, SSM_HEADS), f32)
    m_norm_g = near_one((na, SSM_D_INNER))
    m_w_out = dense((na, SSM_D_INNER, D_MODEL), SSM_D_INNER, DN_BETA)
    kv_w_down = dense((D_MODEL, KV_LORA + QK_ROPE), D_MODEL)
    kv_norm_g = near_one((KV_LORA,))
    kv_w_up = dense((KV_LORA, MLA_HEADS * (QK_NOPE + V_HEAD)), KV_LORA)
    q_w_down = dense((nbl, D_MODEL, Q_LORA), D_MODEL)
    q_norm_g = near_one((nbl, Q_LORA))
    q_w_up = dense((nbl, Q_LORA, MLA_HEADS * (QK_NOPE + QK_ROPE)), Q_LORA)
    o_w = dense((nbl, MLA_HEADS * V_HEAD, D_MODEL), MLA_HEADS * V_HEAD, DN_BETA)
    f_w_in = dense((DEPTH, D_MODEL, 2 * D_FF), D_MODEL)
    f_conv_w = dense((DEPTH, FFN_CONV, 2 * D_FF), FFN_CONV)
    f_conv_b = small((DEPTH, 2 * D_FF))
    f_w_out = dense((DEPTH, D_FF, D_MODEL), D_FF, DN_BETA)
    ln_g = near_one((DEPTH, 2, D_MODEL))
    ln_b = small((DEPTH, 2, D_MODEL), 0.02)
    return {"x": x, "meta_tokens": meta_tokens,
            "m_w_in": m_w_in, "m_conv_w": m_conv_w, "m_conv_b": m_conv_b,
            "m_dt_bias": m_dt_bias, "m_a_log": m_a_log, "m_d": m_d,
            "m_norm_g": m_norm_g, "m_w_out": m_w_out,
            "kv_w_down": kv_w_down, "kv_norm_g": kv_norm_g, "kv_w_up": kv_w_up,
            "q_w_down": q_w_down, "q_norm_g": q_norm_g, "q_w_up": q_w_up, "o_w": o_w,
            "f_w_in": f_w_in, "f_conv_w": f_conv_w, "f_conv_b": f_conv_b, "f_w_out": f_w_out,
            "ln_g": ln_g, "ln_b": ln_b}

def reference(x, meta_tokens, m_w_in, m_conv_w, m_conv_b, m_dt_bias, m_a_log, m_d,
              m_norm_g, m_w_out, kv_w_down, kv_norm_g, kv_w_up, q_w_down, q_norm_g,
              q_w_up, o_w, f_w_in, f_conv_w, f_conv_b, f_w_out, ln_g, ln_b):
    bsz = x.shape[0]
    meta = jnp.broadcast_to(meta_tokens[None].astype(x.dtype), (bsz, N_META, D_MODEL))
    h = jnp.concatenate([meta, x], axis=1)
    cos, sin = rope_tables(h.shape[1])
    k_nope = k_pe = v = None
    for layer in range(DEPTH):
        if layer < N_A_LAYERS:
            i = layer
            mix = mamba2_mixer(h, m_w_in[i], m_conv_w[i], m_conv_b[i], m_dt_bias[i],
                               m_a_log[i], m_d[i], m_norm_g[i], m_w_out[i])
        else:
            j = layer - N_A_LAYERS
            if j == 0:
                k_nope, k_pe, v = mla_shared_kv(h, kv_w_down, kv_norm_g, kv_w_up, cos, sin)
            mix = mla_attention(h, q_w_down[j], q_norm_g[j], q_w_up[j], o_w[j],
                                k_nope, k_pe, v, cos, sin)
        h = layer_norm(DN_ALPHA * h + mix, ln_g[layer, 0], ln_b[layer, 0])
        ffn = conv_ffn(h, f_w_in[layer], f_conv_w[layer], f_conv_b[layer], f_w_out[layer])
        h = layer_norm(DN_ALPHA * h + ffn, ln_g[layer, 1], ln_b[layer, 1])
    return h[:, N_META:]


_drawn_inputs = setup_inputs


def setup_inputs(seed=0):
    import zlib

    import numpy as np

    out = dict(_drawn_inputs(seed))
    spreads = {}
    factors = {'m_conv_b': 8.0, 'm_norm_g': 8.0, 'kv_norm_g': 8.0, 'q_norm_g': 8.0, 'f_conv_b': 8.0}
    for name, (base, spread) in spreads.items():
        noise = np.random.default_rng([zlib.crc32(name.encode()), seed]).standard_normal(out[name].shape)
        drawn = base * np.exp(spread * noise) if base else spread * noise
        out[name] = __import__('jax').numpy.asarray(drawn.astype(out[name].dtype))
    for name, factor in factors.items():
        out[name] = (out[name] * factor).astype(out[name].dtype)
    return out
```

```python
from contextlib import ExitStack

import numpy as np
import concourse.bass as bass
from concourse import mybir

F32 = mybir.dt.float32
F32R = mybir.dt.float32r
ACT = mybir.ActivationFunctionType
ALU = mybir.AluOpType
AX = mybir.AxisListType

P = 128
D = 1024
SEQ = 512
META = 16
T = META + SEQ
HALF = T // 2
BANK = 512
LEFT = BANK - HALF
KT = D // P
ALPHA = float((2.0 * 2) ** 0.25)
LN_EPS = 1e-5
RMS_EPS = 1e-6

CH = [(0, META)] + [(META + P * i, P) for i in range(SEQ // P)]
NC_ = len(CH)

SSM_HEADS, HD, GROUPS, STATE = 32, 64, 4, 128
INNER = SSM_HEADS * HD
GH = SSM_HEADS // GROUPS
GX = INNER // GROUPS // P
GT = 2 + 2 * GX
TAPS, FTAPS = 4, 3

HEADS, NOPE, ROPE, VH = 16, 64, 32, 64
QL, KVL = 384, 256
F = 2816
FT = F // P
SC = float(NOPE + ROPE) ** -0.5

ST = 88
NS = T // ST
assert NS * ST == T and HALF % ST == 0

N_SSM = GROUPS * GT
N_MOUT = KT * (INNER // D)
N_FIN = 2 * FT
N_FOUT = KT * 3
N_DOWN = 7
N_V = 2
N_PAIR = HEADS // 2
N_O = KT
W_SSM = 0
W_MOUT = W_SSM + N_SSM
W_FIN0 = W_MOUT + N_MOUT
W_FOUT0 = W_FIN0 + N_FIN
W_DOWN = W_FOUT0 + N_FOUT
W_V = W_DOWN + N_DOWN
W_PAIR = W_V + N_V
W_O = W_PAIR + N_PAIR
W_FIN1 = W_O + N_O
W_FOUT1 = W_FIN1 + N_FIN
NW = W_FOUT1 + N_FOUT
ST_OF_LN = (GROUPS, GROUPS + 1, GROUPS + 4, GROUPS + 5)
ST_RMS = (GROUPS + 2, GROUPS + 3)
RAW = 4
WT = KT * P


def const_columns():
    at, out = 0, {}
    for name, n in (("ident", P), ("triu", P), ("strict", P), ("wdt", KT * SSM_HEADS),
                    ("dtb", SSM_HEADS), ("alog", SSM_HEADS), ("cw", (N_SSM) * TAPS), ("cb", N_SSM),
                    ("dsk", GROUPS * GX), ("ng", GROUPS * GX), ("fw", 2 * N_FIN * FTAPS),
                    ("fb", 2 * N_FIN), ("lng", 4 * KT), ("lnb", 4 * KT), ("kvg", 2), ("qg", 3),
                    ("neg", 64), ("one", 64)):
        out[name] = (at, at + n)
        at += n
    return out, at


CC, NCON = const_columns()


def build(nc, wstream, xT, consts, tabs, outT, stop=None):
    ctx = ExitStack()
    with ctx:
        def sb(name, shape, dt=F32, c=ctx):
            return c.enter_context(nc.sbuf_tensor(name, shape, dt))

        def sem(name):
            return ctx.enter_context(nc.semaphore(name))

        h = sb("h", [P, KT, T])
        hhi = sb("hhi", [P, KT, T], F32R)
        hlo = sb("hlo", [P, KT, T], F32R)
        raw = sb("raw", [P, RAW, WT])
        whi = sb("whi", [P, 2, WT], F32R)
        wlo = sb("wlo", [P, 2, WT], F32R)
        tmp = sb("tmp", [P, 4, T])
        con = sb("con", [P, NCON])
        ones = sb("ones", [P, P])
        mean_w = sb("mean_w", [P, 4])
        stat = sb("stat", [P, 3, NS])

        def cc(name):
            return con[:, CC[name][0]:CC[name][1]]
        ident, triu, strict = cc("ident"), cc("triu"), cc("strict")
        wdt = cc("wdt").rearrange("p (k n) -> p k n", k=KT)
        cw = cc("cw").rearrange("p (t n) -> p t n", t=N_SSM)
        fw = cc("fw").rearrange("p (t n) -> p t n", t=2 * N_FIN)
        cb, fb, dsk, ng, lng, lnb = (cc(n) for n in ("cb", "fb", "dsk", "ng", "lng", "lnb"))

        ssm = ExitStack()
        ynhi = sb("ynhi", [P, GROUPS * GX, T], F32R, ssm)
        ynlo = sb("ynlo", [P, GROUPS * GX, T], F32R, ssm)
        xy = sb("xy", [P, 2, GX, T], F32, ssm)
        bT = sb("bT", [P, T], F32, ssm)
        cT = sb("cT", [P, T], F32, ssm)
        decay_rhs = sb("decay_rhs", [P, 2, GH * P], F32, ssm)
        btok = sb("btok", [P, P], F32, ssm)
        cbm = sb("cbm", [P, P], F32, ssm)
        xdt = sb("xdt", [P, GH * HD], F32, ssm)
        xw = sb("xw", [P, GH * HD], F32, ssm)
        ytok = sb("ytok", [P, GH * HD], F32, ssm)
        state = sb("state", [P, GH * HD], F32, ssm)
        dtt = sb("dtt", [P, 7, NC_, SSM_HEADS], F32, ssm)
        negA = sb("negA", [P, SSM_HEADS], F32, ssm)
        ssm.close()
        hflat = h[:, :, :].rearrange("p k t -> p (k t)")
        decay = [hflat[:META, 4 * GH * P:4 * GH * P + GH * META].rearrange("p (a l) -> p a l", a=GH)] + [
            hflat[:, i * GH * P:(i + 1) * GH * P].rearrange("p (a l) -> p a l", a=GH) for i in range(4)]
        dt_, acs_, suf_, tot_, a_, wd_, e_ = (dtt[:, i] for i in range(7))

        ffn = ExitStack()
        ahi = sb("ahi", [P, FT, T], F32R, ffn)
        alo = sb("alo", [P, FT, T], F32R, ffn)
        ffn.close()

        att = ExitStack()
        vtok = sb("vtok", [P, NC_, HEADS * VH], F32, att)
        chi = sb("chi", [P, 5, T], F32R, att)
        clo = sb("clo", [P, 5, T], F32R, att)
        craw = sb("craw", [P, 5, T], F32, att)
        tab = sb("tab", [P, 3, T], F32, att)
        kst = sb("kst", [P, 2, T], F32, att)
        qst = sb("qst", [P, 2, T], F32, att)
        prob = sb("prob", [P, 2, T], F32, att)
        probT = sb("probT", [P, 2, NC_, P], F32, att)
        otok = sb("otok", [P, NC_, P], F32, att)
        nmax = sb("nmax", [P, 2, 3], F32, att)
        att.close()

        ps = ctx.enter_context(nc.psum_tensor("ps", [P, 8, BANK], F32))
        psf = ps[:, :, :].rearrange("p b n -> p (b n)")

        def pair(i, half=None):
            at = 2 * i * BANK + LEFT
            return psf[:, at:at + T] if half is None else psf[:, at + HALF * half:at + HALF * (half + 1)]

        names = """att_zero const_in x_in tab_in out_done set_up
            w_hi w_lo w_used
            h_hi0 h_lo0
            dt_mm dt_bias dt_act dt_dve dt_cs dt_exp
            rhs_built decay_mm decay_exp
            conv_first conv_taps conv_silu z_silu
            ssd_in ssd_local ssd_out ytok_ready state_ready ssd_back y_ready
            gate_mul gate_sq
            st_mm sq_used st_eps st_sqrt st_rec st_bc mean_mm mean_cp
            proj_mm conv_tap dt_split yoff state_decay ln_center ln_sq ln_scale ln_hi ln_h ln_lo
            rms_scale rms_hi rms_lo
            h_back out_evac
            ffn_first ffn_silu ffn_mul ffn_hi ffn_lo
            down_copy down_sq kpe v_mm v_evac
            k_evac q_evac s_mm s_max s_exp s_rec pt_mm pt_first pt_rest pv_mm pv_evac ot_mm ot_hi ot_lo""".split()
        S = {n: sem(n) for n in names}
        load = [sem(f"w_load{i}") for i in range(RAW)]
        block = ctx.enter_context(nc.Block())
        STOP = {None: 9, "ssm": 1, "l0": 2, "attn": 3}[stop]
        end = {9: NW, 1: W_FIN0 + 2, 2: W_DOWN + 2, 3: W_FIN1 + 2}[STOP]
        LNH_END = KT * min(STOP, 4)

        @block.sync
        def _(sp):
            def fetch(n, q):
                sp.dma_start(raw[:, n % RAW if isinstance(n, int) else q, :],
                             wstream[bass.ds(n, 1)].rearrange("a p n -> p (a n)") if not isinstance(n, int)
                             else wstream[n]).then_inc(load[q], 16)

            sp.dma_start(h[:, :, :], xT).then_inc(S["x_in"], 16)
            sp.dma_start(con[:, :], consts).then_inc(S["const_in"], 16)
            for n in range(RAW):
                fetch(n, n % RAW)
            full = end // RAW
            with sp.Fori(1, full) as g:
                for q in range(RAW):
                    sp.wait_ge(S["w_lo"], g * RAW + (q - RAW + 1))
                    fetch(g * RAW + q, q)
            for n in range(full * RAW, end):
                sp.wait_ge(S["w_lo"], n - RAW + 1)
                fetch(n, n % RAW)
            sp.wait_ge(S["ln_h"], LNH_END)
            sp.dma_start(outT, h[:, :, META:T]).then_inc(S["out_done"], 16)
            sp.wait_ge(S["out_done"], 16)

        def prep_hi(act, n, q):
            act.wait_ge(load[q], (n - q) * (16 // RAW) + 16)
            if not (isinstance(n, int) and n < 2):
                act.wait_ge(S["w_used"], n - 1)
            nc.scalar.activation(whi[:, q % 2, :], raw[:, q, :], ACT.Copy).then_inc(S["w_hi"], 1)

        def prep_lo(dve, n, q):
            dve.wait_ge(S["w_hi"], n + 1)
            nc.vector.tensor_tensor(wlo[:, q % 2, :], raw[:, q, :], whi[:, q % 2, :].bitcast(F32),
                                    ALU.subtract).then_inc(S["w_lo"], 1)

        def product(slot, nk, xhi, xlo, k0, bank_pair, first=True, last=True, before_k=None, col=0):
            for k in range(nk):
                if before_k is not None:
                    before_k(k)
                for p, (w, x) in enumerate(((whi, xhi), (whi, xlo), (wlo, xhi))):
                    for half in range(2):
                        mm = nc.tensor.matmul(pair(bank_pair, half), w[:, slot, col + k * P:col + (k + 1) * P],
                                              x[:, k0 + k, HALF * half:HALF * (half + 1)],
                                              start=first and k == 0 and p == 0,
                                              stop=last and k == nk - 1 and p == 2)
            return mm

        def stats_mm(pe, tiles, mw, bank, waits, used=None):
            for k, src in enumerate(tiles):
                waits(k)
                for c in range(NS):
                    mm = nc.tensor.matmul(ps[:ST, bank, c:c + 1], src[:, c * ST:(c + 1) * ST],
                                          mean_w[:, mw:mw + 1], start=k == 0 and c == 0, stop=k == len(tiles) - 1,
                                          skip_group_check=True)
                    if used is not None and c == NS - 1 and k < len(tiles) - 4:
                        mm.then_inc(used, 1)
            return mm

        def broadcast_mm(which, bank_pair):
            for c in range(NS):
                at = 2 * bank_pair * BANK + LEFT + c * ST
                mm = nc.tensor.matmul(psf[:, at:at + ST], stat[:ST, which, c:c + 1].broadcast_to([ST, P]),
                                      ident[:ST, :ST], start=True, stop=True)
            return mm

        def stat_ps(bank):
            return ps[:ST, bank, 0:NS]

        def ln_pe(pe, L):
            pe.wait_ge(S["out_evac"], 2 + KT * (L + 1))
            stats_mm(pe, [h[:, k, :] for k in range(KT)], 0, 4, lambda k: None).then_inc(S["mean_mm"], 1)
            pe.wait_ge(S["mean_cp"], L + 1)
            broadcast_mm(0, 0).then_inc(S["mean_mm"], 1)
            stats_mm(pe, [tmp[:, k % 4, :] for k in range(KT)], 0, 5,
                     lambda k: pe.wait_ge(S["ln_sq"], KT * L + k + 1), S["sq_used"]).then_inc(S["st_mm"], 1)
            pe.wait_ge(S["st_rec"], ST_OF_LN[L] + 1)
            broadcast_mm(2, 1).then_inc(S["st_bc"], 1)

        def ln_act(act, L):
            for k in range(KT):
                act.wait_ge(S["ln_center"], KT * L + k + 1)
                if k >= 4:
                    act.wait_ge(S["sq_used"], 4 * L + k - 3)
                nc.scalar.activation(tmp[:, k % 4, :], h[:, k, :], ACT.Square).then_inc(S["ln_sq"], 1)
            act.wait_ge(S["st_eps"], ST_OF_LN[L] + 1)
            nc.scalar.activation(stat[:ST, 1, :], stat[:ST, 1, :], ACT.Sqrt).then_inc(S["st_sqrt"], 1)
            for k in range(KT):
                j = L * KT + k
                act.wait_ge(S["ln_scale"], j + 1)
                if L < 3:
                    nc.scalar.activation(hhi[:, k, :], h[:, k, :], ACT.Identity, bias=lnb[:, j:j + 1],
                                         scale=lng[:, j:j + 1]).then_inc(S["ln_hi"], 1)
                nc.scalar.activation(h[:, k, :], h[:, k, :], ACT.Identity, bias=lnb[:, j:j + 1],
                                     scale=lng[:, j:j + 1]).then_inc(S["ln_h"], 1)

        def ln_dve(dve, L):
            dve.wait_ge(S["mean_mm"], 2 * L + 1)
            nc.vector.tensor_copy(stat[:ST, 0, :], stat_ps(4)).then_inc(S["mean_cp"], 1)
            dve.wait_ge(S["mean_mm"], 2 * L + 2)
            for k in range(KT):
                nc.vector.tensor_tensor(h[:, k, :], h[:, k, :], pair(0), ALU.subtract).then_inc(S["ln_center"], 1)
            finish_stat(dve, ST_OF_LN[L], 5, LN_EPS)
            for k in range(KT):
                dve.wait_ge(S["ln_sq"], KT * L + KT)
                nc.vector.tensor_tensor(h[:, k, :], h[:, k, :], pair(1), ALU.mult).then_inc(S["ln_scale"], 1)
            if L < 3:
                for k in range(KT):
                    dve.wait_ge(S["ln_h"], KT * L + k + 1)
                    nc.vector.tensor_tensor(hlo[:, k, :], h[:, k, :], hhi[:, k, :].bitcast(F32),
                                            ALU.subtract).then_inc(S["ln_lo"], 1)

        def finish_stat(dve, n, bank, eps):
            dve.wait_ge(S["st_mm"], n + 1)
            nc.vector.tensor_scalar(stat[:ST, 1, :], stat_ps(bank), eps, None, ALU.add).then_inc(S["st_eps"], 1)
            dve.wait_ge(S["st_sqrt"], n + 1)
            nc.vector.reciprocal(stat[:ST, 2, :], stat[:ST, 1, :]).then_inc(S["st_rec"], 1)
            dve.wait_ge(S["st_bc"], n + 1)

        SSD_AFTER_Z = [["in0"], ["out0", "in1"], ["back0", "out1", "in2"], ["back1", "out2", "in3"],
                       ["back2", "out3", "in4", "back3", "out4", "back4"]]

        def ssd_steps(run):
            for z, stages in enumerate(SSD_AFTER_Z):
                for s in stages:
                    run(s[:-1], int(s[-1]))
                if z < GX:
                    run("z", z)

        def ssm_pe(pe):
            pe.wait_ge(S["const_in"], 16)
            pe.wait_ge(S["x_in"], 16)
            for c, (t0, n) in enumerate(CH):
                for k in range(KT):
                    mm = nc.tensor.matmul(ps[:n, 4, c * SSM_HEADS:(c + 1) * SSM_HEADS], h[:, k, t0:t0 + n],
                                          wdt[:, k, :], start=k == 0, stop=k == KT - 1)
            mm.then_inc(S["dt_mm"], 1)
            pe.wait_ge(S["dt_dve"], DT_STEPS)
            pe.wait_ge(S["set_up"], 7)
            for b, left in ((5, triu), (6, strict), (7, ones)):
                m0 = P if b == 7 else META
                nc.tensor.matmul(ps[:m0, b, 0:SSM_HEADS], left[:META, :m0], a_[:META, 0, :], start=True, stop=True)
                mm = nc.tensor.matmul(ps[:, b, SSM_HEADS:NC_ * SSM_HEADS], left[:, :], a_[:, 1:, :],
                                      start=True, stop=True)
                mm.then_inc(S["dt_cs"] if b == 5 else S["decay_mm"], 1)
            pe.wait_ge(S["dt_exp"], 5)
            with pe.Fori(0, GROUPS // 2) as it:
                for q in range(2):
                    ssm_group_pe(pe, it * 2 + q, q)
                norm_pe_sum(pe, it * 2 + 1)
                norm_pe_spread(pe, it * 2 + 1)
                pe.wait_ge(S["rms_scale"], it * (2 * GX) + 2 * GX)

        def ssm_group_pe(pe, g, q):
            for c, (t0, n) in enumerate(CH):
                u = g * NC_ + c
                pe.wait_ge(S["rhs_built"], u + 1)
                if c >= 2:
                    pe.wait_ge(S["decay_exp"], u - 1)
                slot = (q * NC_ + c) % 2
                b = 4 + 2 * (c % 2)
                if c == 0:
                    mm = nc.tensor.matmul(ps[:, b, 0:GH * n], strict[:n, :], decay_rhs[:n, slot, 0:GH * n],
                                          start=True, stop=True)
                else:
                    for half in range(2):
                        mm = nc.tensor.matmul(ps[:, b + half, :], strict[:, :],
                                              decay_rhs[:, slot, half * BANK:(half + 1) * BANK],
                                              start=True, stop=True)
                mm.then_inc(S["decay_mm"], 1)
            for j in range(2 + GX):
                n = g * GT + j
                pe.wait_ge(S["w_lo"], n + 1)
                if j >= 2:
                    pe.wait_ge(S["conv_taps"], g * (2 + GX) + (j - 1))
                elif q == 1 and j == 0:
                    pe.wait_ge(S["z_silu"], g * GX)
                elif q == 1 and j == 1:
                    pe.wait_ge(S["y_ready"], g * (NC_ * GX))
                product(j % 2, KT, hhi, hlo, 0, j % 2,
                        before_k=(lambda k: pe.wait_ge(S["h_lo0"], k + 1)) if j == 0 else None
                        ).then_inc(S["w_used"], 1)
                if q == 1 and j == 0:
                    pe.wait_ge(S["decay_exp"], g * NC_ + NC_)
                    norm_pe_sum(pe, g - 1)
                if q == 1 and j == 2:
                    norm_pe_spread(pe, g - 1)
            pe.wait_ge(S["conv_silu"], g * (2 + GX) + 2 + GX)
            if q == 1:
                pe.wait_ge(S["rms_scale"], g * GX)
            pe.wait_ge(S["decay_exp"], g * NC_ + NC_)

            def run(kind, c):
                u = g * NC_ + c
                if kind == "z":
                    n = g * GT + 2 + GX + c
                    pe.wait_ge(S["w_lo"], n + 1)
                    if c > 0:
                        pe.wait_ge(S["z_silu"], g * GX + c)
                    product(c % 2, KT, hhi, hlo, 0, 0).then_inc(S["w_used"], 1)
                    return
                t0, n = CH[c]
                if kind == "in":
                    if c > 0:
                        pe.wait_ge(S["ssd_local"], u * 5)
                    for j in range(GX):
                        nc.tensor.transpose(ps[:n, 4, j * P:(j + 1) * P], xy[:, q, j, t0:t0 + n], ident)
                    nc.tensor.transpose(ps[:n, 5, 0:P], bT[:, t0:t0 + n], ident)
                    nc.tensor.matmul(ps[:n, 5, P:P + n], bT[:, t0:t0 + n], cT[:, t0:t0 + n],
                                     start=True, stop=True).then_inc(S["ssd_in"], 1)
                elif kind == "out":
                    pe.wait_ge(S["ssd_local"], u * 5 + 5)
                    if c > 0:
                        pe.wait_ge(S["ytok_ready"], u)
                        pe.wait_ge(S["state_ready"], g * (NC_ - 1) + c)
                    if c < NC_ - 1:
                        mm = nc.tensor.matmul(ps[:, 2, :], btok[:n, :], xw[:n, :], start=True, stop=True)
                    for a in range(GH):
                        mm = nc.tensor.matmul(ps[:n, 6, a * HD:(a + 1) * HD], decay[c][:n, a, :n],
                                              xdt[:n, a * HD:(a + 1) * HD], start=True, stop=True)
                    if c > 0:
                        mm = nc.tensor.matmul(ps[:n, 7, :], cT[:, t0:t0 + n], state[:, :], start=True, stop=True)
                    mm.then_inc(S["ssd_out"], 1)
                else:
                    pe.wait_ge(S["ytok_ready"], u + 1)
                    if c > 0:
                        pe.wait_ge(S["y_ready"], u * GX)
                    for j in range(GX):
                        mm = nc.tensor.transpose(ps[:, 3, j * P:(j + 1) * P], ytok[:, j * P:(j + 1) * P], ident)
                    mm.then_inc(S["ssd_back"], 1)
            ssd_steps(run)

        def norm_pe_sum(pe, g):
            stats_mm(pe, [tmp[:, j, :] for j in range(GX)], 1, 6,
                     lambda j: pe.wait_ge(S["gate_sq"], g * GX + j + 1)).then_inc(S["st_mm"], 1)

        def norm_pe_spread(pe, g):
            pe.wait_ge(S["st_rec"], g + 1)
            broadcast_mm(2, 2).then_inc(S["st_bc"], 1)

        DT_STEPS = 6

        def ssm_act(act):
            act.wait_ge(S["x_in"], 16)
            for k in range(KT):
                nc.scalar.activation(hhi[:, k, :], h[:, k, :], ACT.Copy).then_inc(S["h_hi0"], 1)
                if k < 2:
                    prep_hi(act, k, k)
            act.wait_ge(S["const_in"], 16)
            act.wait_ge(S["dt_bias"], 2)
            nc.scalar.activation(e_, dt_, ACT.Abs).then_inc(S["dt_act"], 1)
            act.wait_ge(S["dt_act"], 1)
            nc.scalar.activation(e_, e_, ACT.Exp, scale=-1.0).then_inc(S["dt_act"], 1)
            nc.scalar.activation(negA[:, :], cc("alog"), ACT.Exp).then_inc(S["dt_act"], 1)
            act.wait_ge(S["dt_dve"], 1)
            nc.scalar.activation(suf_, tot_, ACT.Ln).then_inc(S["dt_act"], 1)
            act.wait_ge(S["decay_mm"], 2)
            act.wait_ge(S["dt_cs"], 1)
            acs_ps = ps[:, 5, 0:NC_ * SSM_HEADS].rearrange("p (c n) -> p c n", c=NC_)
            suf_ps = ps[:, 6, 0:NC_ * SSM_HEADS].rearrange("p (c n) -> p c n", c=NC_)
            tot_ps = ps[:, 7, 0:NC_ * SSM_HEADS].rearrange("p (c n) -> p c n", c=NC_)
            for to, frm in ((acs_[:META, 0], acs_ps[:META, 0]), (acs_[:, 1:], acs_ps[:, 1:]),
                            (suf_[:META, 0], suf_ps[:META, 0]), (suf_[:, 1:], suf_ps[:, 1:]), (tot_, tot_ps)):
                nc.scalar.activation(to, frm, ACT.Exp).then_inc(S["dt_exp"], 1)
            act.wait_ge(S["h_lo0"], KT)
            with act.Fori(0, GROUPS // 2) as it:
                for q in range(2):
                    ssm_group_act(act, it * 2 + q, q)
                norm_act_sq(act, it * 2 + 1, 1)
                norm_act_sqrt(act, it * 2 + 1)
                norm_act_hi(act, it * 2 + 1, 1)

        def ssm_group_act(act, g, q):
            for c, (t0, n) in enumerate(CH):
                act.wait_ge(S["decay_mm"], g * NC_ + c + 3)
                b = 4 + 2 * (c % 2)
                src = ps[:n, b, 0:GH * n] if c == 0 else psf[:, b * BANK:(b + 2) * BANK]
                nc.scalar.activation(decay[c], src.rearrange("p (a l) -> p a l", a=GH), ACT.Exp
                                     ).then_inc(S["decay_exp"], 1)
            if q == 1:
                norm_act_sq(act, g - 1, 0)
            dst = [bT[:, :], cT[:, :]] + [xy[:, q, j, :] for j in range(GX)]

            def silu(j):
                act.wait_ge(S["conv_taps"], g * (2 + GX) + j + 1)
                nc.scalar.activation(dst[j], dst[j], ACT.Silu).then_inc(S["conv_silu"], 1)

            for j in range(2 + GX):
                n = g * GT + j
                prep_hi(act, n + 2, (q * GT + j + 2) % RAW)
                act.wait_ge(S["w_used"], n + 1)
                nc.scalar.activation(dst[j], pair(j % 2), ACT.Identity, bias=cb[:, bass.ds(n, 1)],
                                     scale=cw[:, bass.ds(n, 1), TAPS - 1]).then_inc(S["conv_first"], 1)
                if j > 0:
                    silu(j - 1)
                if q == 1 and j == 1:
                    norm_act_sqrt(act, g - 1)
                if q == 1 and j == 3:
                    norm_act_hi(act, g - 1, 0)
            silu(1 + GX)
            for j in range(GX):
                n = g * GT + 2 + GX + j
                prep_hi(act, n + 2, (q * GT + 4 + GX + j) % RAW)
                act.wait_ge(S["w_used"], n + 1)
                nc.scalar.activation(tmp[:, j, :], pair(0), ACT.Silu).then_inc(S["z_silu"], 1)

        def norm_act_sq(act, g, q):
            for j in range(GX):
                act.wait_ge(S["gate_mul"], g * GX + j + 1)
                nc.scalar.activation(tmp[:, j, :], xy[:, q, j, :], ACT.Square).then_inc(S["gate_sq"], 1)

        def norm_act_sqrt(act, n):
            act.wait_ge(S["st_eps"], n + 1)
            nc.scalar.activation(stat[:ST, 1, :], stat[:ST, 1, :], ACT.Sqrt).then_inc(S["st_sqrt"], 1)

        def norm_act_hi(act, g, q):
            for j in range(GX):
                act.wait_ge(S["rms_scale"], g * GX + j + 1)
                nc.scalar.activation(ynhi[:, bass.ds(g * GX + j, 1), :], xy[:, q, j:j + 1, :], ACT.Copy,
                                     scale=ng[:, bass.ds(g * GX + j, 1)]).then_inc(S["rms_hi"], 1)

        def ssm_pool(pool):
            pool.wait_ge(S["const_in"], 16)
            pool.wait_ge(S["dt_dve"], DT_STEPS)
            with pool.Fori(0, GROUPS // 2) as it:
                for q in range(2):
                    for c, (t0, n) in enumerate(CH):
                        u = it * (2 * NC_) + q * NC_ + c
                        pool.wait_ge(S["decay_mm"], u + 1)
                        out = decay_rhs[:n, u_slot(q, c), 0:GH * n].rearrange("p (a l) -> p a l", a=GH)
                        nc.gpsimd.tensor_tensor(
                            out, a_[:n, c, bass.ds(it * (2 * GH) + q * GH, GH)].unsqueeze(2).broadcast_to([n, GH, n]),
                            triu[:n, :n].unsqueeze(1).broadcast_to([n, GH, n]), ALU.mult
                        ).then_inc(S["rhs_built"], 1)

        def u_slot(q, c):
            return (q * NC_ + c) % 2

        def ssm_dve(dve):
            nc.vector.memset(ones[:, :], 1.0).then_inc(S["set_up"], 1)
            for i, n in enumerate((D, INNER // GROUPS, KVL, QL)):
                nc.vector.memset(mean_w[:, i:i + 1], 1.0 / n).then_inc(S["set_up"], 1)
            nc.vector.memset(dtt[:, :, :, :], 0.0).then_inc(S["set_up"], 1)
            nc.vector.memset(ytok[:, :], 0.0).then_inc(S["set_up"], 1)
            for k in range(KT):
                dve.wait_ge(S["h_hi0"], k + 1)
                nc.vector.tensor_tensor(hlo[:, k, :], h[:, k, :], hhi[:, k, :].bitcast(F32), ALU.subtract
                                        ).then_inc(S["h_lo0"], 1)
                if k < 2:
                    prep_lo(dve, k, k)
            dve.wait_ge(S["const_in"], 16)
            dve.wait_ge(S["set_up"], 7)
            dve.wait_ge(S["dt_mm"], 1)
            dtb = cc("dtb")
            dt_ps = ps[:, 4, 0:NC_ * SSM_HEADS].rearrange("p (c n) -> p c n", c=NC_)
            nc.vector.tensor_tensor(dt_[:META, 0], dt_ps[:META, 0], dtb[:META], ALU.add).then_inc(S["dt_bias"], 1)
            nc.vector.tensor_tensor(dt_[:, 1:], dt_ps[:, 1:], dtb.unsqueeze(1).broadcast_to([P, NC_ - 1, SSM_HEADS]),
                                    ALU.add).then_inc(S["dt_bias"], 1)
            dve.wait_ge(S["dt_act"], 2)
            nc.vector.tensor_scalar(tot_, e_, 1.0, None, ALU.add).then_inc(S["dt_dve"], 1)
            dve.wait_ge(S["dt_dve"], 1)
            nc.vector.scalar_tensor_tensor(acs_, tot_, -1.0, e_, ALU.add, ALU.subtract).then_inc(S["dt_dve"], 1)
            dve.wait_ge(S["dt_act"], 4)
            dve.wait_ge(S["dt_dve"], 2)
            nc.vector.tensor_tensor(suf_, suf_, acs_, ALU.subtract).then_inc(S["dt_dve"], 1)
            dve.wait_ge(S["dt_dve"], 3)
            nc.vector.scalar_tensor_tensor(dt_, dt_, 0.0, suf_, ALU.max, ALU.add).then_inc(S["dt_dve"], 1)
            dve.wait_ge(S["dt_dve"], 4)
            nc.vector.tensor_scalar(negA[:, :], negA[:, :], -1.0, None, ALU.mult).then_inc(S["dt_dve"], 1)
            dve.wait_ge(S["dt_dve"], 5)
            nc.vector.tensor_tensor(a_, dt_, negA[:, :].unsqueeze(1).broadcast_to([P, NC_, SSM_HEADS]),
                                    ALU.mult).then_inc(S["dt_dve"], 1)
            dve.wait_ge(S["dt_exp"], 5)
            nc.vector.tensor_tensor(wd_, dt_, suf_, ALU.mult).then_inc(S["dt_split"], 1)
            dve.wait_ge(S["dt_split"], 1)
            with dve.Fori(0, GROUPS // 2) as it:
                for q in range(2):
                    ssm_group_dve(dve, it * 2 + q, q)
                norm_dve_gate(dve, it * 2 + 1, 1)
                finish_stat(dve, it * 2 + 1, 6, RMS_EPS)
                norm_dve_scale(dve, it * 2 + 1, 1)
            for half in range(2):
                nc.vector.tensor_tensor(h[:, 4 * half:4 * half + 4, :], hhi[:, 4 * half:4 * half + 4, :].bitcast(F32),
                                        hlo[:, 4 * half:4 * half + 4, :].bitcast(F32), ALU.add
                                        ).then_inc(S["out_evac"], 1)

        def taps(dve, dst, bank_pair, weight, ntaps, tap_count):
            for i in range(1, ntaps):
                if i > 1:
                    dve.wait_ge(S["conv_tap"], tap_count + i - 1)
                op = nc.vector.scalar_tensor_tensor(dst[:, i:T], pair(bank_pair)[:, 0:T - i], weight(i), dst[:, i:T],
                                                    ALU.mult, ALU.add)
                op.then_inc(S["conv_taps"] if i == ntaps - 1 else S["conv_tap"], 1)

        def head_scale(n, per_head):
            return per_head.unsqueeze(2).broadcast_to([n, GH, HD])

        def heads(ap):
            return ap.rearrange("p (a d) -> p a d", a=GH)

        def ssm_group_dve(dve, g, q):
            dst = [bT[:, :], cT[:, :]] + [xy[:, q, j, :] for j in range(GX)]
            if q == 1:
                norm_dve_gate(dve, g - 1, 0)
            for j in range(2 + GX):
                n = g * GT + j
                prep_lo(dve, n + 2, (q * GT + j + 2) % RAW)
                dve.wait_ge(S["conv_first"], g * (2 + GX) + j + 1)
                taps(dve, dst[j], j % 2, lambda i: cw[:, bass.ds(n, 1), TAPS - 1 - i], TAPS,
                     (g * (2 + GX) + j) * (TAPS - 2))
                if q == 1 and j == 1:
                    finish_stat(dve, g - 1, 6, RMS_EPS)
                if q == 1 and j == 2:
                    norm_dve_scale(dve, g - 1, 0)

            def run(kind, c):
                u = g * NC_ + c
                if kind == "z":
                    n = g * GT + 2 + GX + c
                    prep_lo(dve, n + 2, (q * GT + 4 + GX + c) % RAW)
                    return
                t0, n = CH[c]
                gh = bass.ds(g * GH, GH)
                done = S["ssd_local"]
                if kind == "in":
                    dve.wait_ge(S["ssd_in"], u + 1)
                    nc.vector.tensor_tensor(cbm[:n, :n], ps[:n, 5, P:P + n], triu[:n, :n], ALU.mult).then_inc(done, 1)
                    nc.vector.tensor_copy(btok[:n, :], ps[:n, 5, 0:P]).then_inc(done, 1)
                    nc.vector.tensor_tensor(heads(xdt[:n, :]), heads(ps[:n, 4, :]), head_scale(n, dt_[:n, c, gh]),
                                            ALU.mult).then_inc(done, 1)
                    nc.vector.tensor_tensor(heads(xw[:n, :]), heads(ps[:n, 4, :]), head_scale(n, wd_[:n, c, gh]),
                                            ALU.mult).then_inc(done, 1)
                    dve.wait_ge(S["decay_exp"], u + 1)
                    dve.wait_ge(done, u * 5 + 1)
                    nc.vector.tensor_tensor(decay[c], decay[c], cbm[:n, :n].unsqueeze(1).broadcast_to([n, GH, n]),
                                            ALU.mult).then_inc(done, 1)
                elif kind == "out":
                    dve.wait_ge(S["ssd_out"], u + 1)
                    if c == 0:
                        nc.vector.tensor_copy(ytok[:n, :], ps[:n, 6, :]).then_inc(S["ytok_ready"], 1)
                        nc.vector.tensor_copy(state[:, :], ps[:, 2, :]).then_inc(S["state_ready"], 1)
                        return
                    if c > 0:
                        nc.vector.tensor_tensor(heads(ytok[:n, :]), heads(ps[:n, 7, :]),
                                                head_scale(n, acs_[:n, c, gh]), ALU.mult).then_inc(S["yoff"], 1)
                    if c < NC_ - 1:
                        nc.vector.tensor_tensor(heads(state[:, :]), heads(state[:, :]),
                                                head_scale(P, tot_[:, c, gh]), ALU.mult).then_inc(S["state_decay"], 1)
                    dve.wait_ge(S["yoff"], g * (NC_ - 1) + c)
                    nc.vector.tensor_tensor(ytok[:n, :], ytok[:n, :], ps[:n, 6, :], ALU.add
                                            ).then_inc(S["ytok_ready"], 1)
                    if c < NC_ - 1:
                        dve.wait_ge(S["state_decay"], g * (NC_ - 2) + c)
                        nc.vector.tensor_tensor(state[:, :], state[:, :], ps[:, 2, :], ALU.add
                                                ).then_inc(S["state_ready"], 1)
                else:
                    dve.wait_ge(S["ssd_back"], u + 1)
                    for j in range(GX):
                        nc.vector.scalar_tensor_tensor(xy[:, q, j, t0:t0 + n], xy[:, q, j, t0:t0 + n],
                                                       dsk[:, bass.ds(g * GX + j, 1)], ps[:, 3, j * P:j * P + n],
                                                       ALU.mult, ALU.add).then_inc(S["y_ready"], 1)
            ssd_steps(run)

        def norm_dve_gate(dve, g, q):
            dve.wait_ge(S["y_ready"], g * (NC_ * GX) + NC_ * GX)
            for j in range(GX):
                dve.wait_ge(S["z_silu"], g * GX + j + 1)
                nc.vector.tensor_tensor(xy[:, q, j, :], xy[:, q, j, :], tmp[:, j, :], ALU.mult
                                        ).then_inc(S["gate_mul"], 1)

        def norm_dve_scale(dve, g, q):
            for j in range(GX):
                dve.wait_ge(S["gate_sq"], g * GX + j + 1)
                nc.vector.tensor_tensor(xy[:, q, j, :], xy[:, q, j, :], pair(2), ALU.mult
                                        ).then_inc(S["rms_scale"], 1)
            for j in range(GX):
                dve.wait_ge(S["rms_hi"], g * GX + j + 1)
                nc.vector.scalar_tensor_tensor(
                    ynlo[:, bass.ds(g * GX + j, 1), :], xy[:, q, j:j + 1, :], ng[:, bass.ds(g * GX + j, 1)],
                    ynhi[:, bass.ds(g * GX + j, 1), :].bitcast(F32), ALU.mult, ALU.subtract).then_inc(S["rms_lo"], 1)

        def out_steps(base, per, out0, body, run, straight=False, loop=None):
            def step(it):
                for m in range(body):
                    for s in range(per):
                        idx = m * per + s
                        run(base + it * (body * per) + idx, (base + idx) % RAW, it * body + m, m, s)
            if straight:
                for it in range(KT // body):
                    step(it)
            else:
                with loop(0, KT // body) as it:
                    step(it)

        def out_pe(pe, base, per, number, sizes, xhi, xlo, body, straight, ready):
            ready()
            def run(n, pos, m, mq, s):
                pe.wait_ge(S["w_lo"], n + 1)
                if s == 0:
                    pe.wait_ge(S["out_evac"], m + (KT * number + 1))
                product(pos % 2, sizes[s], xhi, xlo, KT * s, mq % 2, s == 0, s == per - 1
                        ).then_inc(S["w_used"], 1)
            out_steps(base, per, number, body, run, straight, pe.Fori)

        def out_act(act, base, per, body, straight):
            def run(n, pos, m, mq, s):
                if not isinstance(n, int) or n + 2 < end:
                    prep_hi(act, n + 2, (pos + 2) % RAW)
            out_steps(base, per, 0, body, run, straight, act.Fori)

        def out_dve(dve, base, per, body, straight):
            def run(n, pos, m, mq, s):
                if not isinstance(n, int) or n + 2 < end:
                    prep_lo(dve, n + 2, (pos + 2) % RAW)
                if s == per - 1:
                    dve.wait_ge(S["w_used"], n + 1)
                    hm = h[:, bass.ds(m, 1), :] if not isinstance(m, int) else h[:, m:m + 1, :]
                    nc.vector.scalar_tensor_tensor(hm, hm, ALPHA, pair(mq % 2).unsqueeze(1), ALU.mult, ALU.add
                                                   ).then_inc(S["out_evac"], 1)
            out_steps(base, per, 0, body, run, straight, dve.Fori)

        def ffn_pe(pe, L, base):
            with pe.Fori(0, N_FIN // 4) as it:
                for q in range(4):
                    n = base + it * 4 + q
                    pe.wait_ge(S["w_lo"], n + 1)
                    pe.wait_ge(S["conv_taps"], it * 4 + (TAP0 + L * N_FIN + q - 1))
                    product((base + q) % 2, KT, hhi, hlo, 0, q % 2,
                            before_k=(lambda k: pe.wait_ge(S["ln_lo"], KT * LN_OF_FFN[L] + k + 1)) if q == 0 else None
                            ).then_inc(S["w_used"], 1)

        def ffn_act(act, L, base):
            with act.Fori(0, N_FIN // 4) as it:
                for q in range(4):
                    n = base + it * 4 + q
                    v = it * 4 + (L * N_FIN + q)
                    prep_hi(act, n + 2, (base + q + 2) % RAW)
                    act.wait_ge(S["w_used"], n + 1)
                    nc.scalar.activation(tmp[:, q, :], pair(q % 2), ACT.Identity, bias=fb[:, bass.ds(v, 1)],
                                         scale=fw[:, bass.ds(v, 1), FTAPS - 1]).then_inc(S["conv_first"], 1)
                    if q % 2:
                        j = it * 2 + (L * FT + q // 2)
                        act.wait_ge(S["conv_taps"], v + TAP0)
                        nc.scalar.activation(tmp[:, q - 1, :], tmp[:, q - 1, :], ACT.Silu).then_inc(S["ffn_silu"], 1)
                        act.wait_ge(S["ffn_mul"], j + 1)
                        nc.scalar.activation(ahi[:, bass.ds(it * 2 + q // 2, 1), :], tmp[:, q - 1:q, :], ACT.Copy
                                             ).then_inc(S["ffn_hi"], 1)

        def ffn_dve(dve, L, base):
            with dve.Fori(0, N_FIN // 4) as it:
                for q in range(4):
                    n = base + it * 4 + q
                    v = it * 4 + (L * N_FIN + q)
                    prep_lo(dve, n + 2, (base + q + 2) % RAW)
                    dve.wait_ge(S["conv_first"], v + TAP0 + 1)
                    taps(dve, tmp[:, q, :], q % 2, lambda i: fw[:, bass.ds(v, 1), FTAPS - 1 - i], FTAPS,
                         v * (FTAPS - 2) + TAP0 * (TAPS - 2))
                    if q % 2:
                        j = it * 2 + (L * FT + q // 2)
                        dve.wait_ge(S["ffn_silu"], j + 1)
                        dve.wait_ge(S["conv_taps"], v + TAP0 + 1)
                        nc.vector.tensor_tensor(tmp[:, q - 1, :], tmp[:, q - 1, :], tmp[:, q, :], ALU.mult
                                                ).then_inc(S["ffn_mul"], 1)
                        dve.wait_ge(S["ffn_hi"], j + 1)
                        jl = bass.ds(it * 2 + q // 2, 1)
                        nc.vector.tensor_tensor(alo[:, jl, :], tmp[:, q - 1:q, :], ahi[:, jl, :].bitcast(F32),
                                                ALU.subtract).then_inc(S["ffn_lo"], 1)

        TAP0 = GROUPS * (2 + GX)
        LN_OF_FFN = (0, 2)
        fout = (KT, KT, FT - 2 * KT)

        N_CKV, N_CQ = KVL // P, QL // P
        N_C = N_CKV + N_CQ
        SQ = [tmp[:, i, :] for i in range(4)] + [qst[:, 0, :]]
        DOWN_LN = 1

        def down_pe(pe):
            for t in range(N_DOWN):
                n = W_DOWN + t
                pe.wait_ge(S["w_lo"], n + 1)
                if t >= 2:
                    if t - 2 < N_C:
                        pe.wait_ge(S["down_copy"], t - 1)
                product(n % 2, KT, hhi, hlo, 0, t % 2,
                        before_k=(lambda k: pe.wait_ge(S["ln_lo"], KT * DOWN_LN + k + 1)) if t == 0 else None
                        ).then_inc(S["w_used"], 1)
            for i, (t0, t1) in enumerate(((0, N_CKV), (N_CKV, N_C))):
                stats_mm(pe, SQ[t0:t1], 2 + i, 4 + i, lambda k: pe.wait_ge(S["down_sq"], t0 + k + 1)
                         ).then_inc(S["st_mm"], 1)
            for i, first in enumerate((0, N_CKV)):
                pe.wait_ge(S["st_rec"], ST_RMS[i] + 1)
                if i:
                    pe.wait_ge(S["rms_scale"], GROUPS * GX + first)
                broadcast_mm(2, 3).then_inc(S["st_bc"], 1)
            pe.wait_ge(S["w_lo"], W_V + N_V)
            pe.wait_ge(S["rms_lo"], GROUPS * GX + N_CKV)
            pe.wait_ge(S["kpe"], 2)
            pe.wait_ge(S["down_copy"], N_C)
            for v in range(2 * NC_):
                t0, half = CH[v // 2][0], v % 2
                if v >= 4:
                    pe.wait_ge(S["v_evac"], v - 3)
                for kt in range(N_V):
                    slot = (W_V + kt) % 2
                    for p, (x, w) in enumerate(((chi, whi), (clo, whi), (chi, wlo))):
                        mm = nc.tensor.matmul(ps[:, v % 4, :], x[:, kt, t0:t0 + P],
                                              w[:, slot, half * BANK:(half + 1) * BANK],
                                              start=kt == 0 and p == 0, stop=kt == N_V - 1 and p == 2)
                    if v == 2 * NC_ - 1:
                        mm.then_inc(S["w_used"], 1)
                if v < 2 * NC_ - 1:
                    mm.then_inc(S["v_mm"], 1)

        def down_act(act):
            for t in range(N_DOWN):
                n = W_DOWN + t
                prep_hi(act, n + 2, (n + 2) % RAW)
                if t < N_C:
                    act.wait_ge(S["w_used"], n + 1)
                    nc.scalar.activation(craw[:, t, :], pair(t % 2), ACT.Copy).then_inc(S["down_copy"], 1)
                    act.wait_ge(S["down_copy"], t + 1)
                    nc.scalar.activation(SQ[t], craw[:, t, :], ACT.Square).then_inc(S["down_sq"], 1)
            for i, (t0, t1) in enumerate(((0, N_CKV), (N_CKV, N_C))):
                norm_act_sqrt(act, ST_RMS[i])
                for t in range(t0, t1):
                    act.wait_ge(S["rms_scale"], GROUPS * GX + t + 1)
                    gain = cc("kvg")[:, t:t + 1] if i == 0 else cc("qg")[:, t - t0:t - t0 + 1]
                    nc.scalar.activation(chi[:, t, :], craw[:, t, :], ACT.Copy, scale=gain).then_inc(S["rms_hi"], 1)
            act.wait_ge(S["att_zero"], 2)
            for v in range(2 * NC_):
                t0, n = CH[v // 2]
                act.wait_ge(*((S["v_mm"], v + 1) if v < 2 * NC_ - 1 else (S["w_used"], W_PAIR)))
                nc.scalar.activation(vtok[:n, v // 2, (v % 2) * BANK:(v % 2 + 1) * BANK], ps[:n, v % 4, :], ACT.Copy
                                     ).then_inc(S["v_evac"], 1)
            for i in range(N_V):
                prep_hi(act, W_PAIR + i, (W_PAIR + i) % RAW)

        def down_dve(dve):
            nc.vector.memset(probT[:, :, 0, :], 0.0).then_inc(S["att_zero"], 1)
            nc.vector.memset(vtok[:, 0, :], 0.0).then_inc(S["att_zero"], 1)
            for t in range(N_DOWN):
                n = W_DOWN + t
                prep_lo(dve, n + 2, (n + 2) % RAW)
                if t >= N_C:
                    if t == N_C:
                        dve.wait_ge(S["tab_in"], 16)
                    dve.wait_ge(S["w_used"], n + 1)
                    nc.vector.tensor_tensor(kst[NOPE:, t - N_C, :], pair(t % 2)[NOPE:], tab[NOPE:, 1 + t - N_C, :],
                                            ALU.mult).then_inc(S["kpe"], 1)
            dve.wait_ge(S["kpe"], 2)
            nc.vector.tensor_tensor(kst[NOPE:, 0, :], kst[NOPE:, 0, :], kst[NOPE:, 1, :], ALU.add
                                    ).then_inc(S["kpe"], 1)
            dve.wait_ge(S["kpe"], 3)
            nc.vector.tensor_copy(kst[NOPE:, 1, :], kst[NOPE:, 0, :]).then_inc(S["kpe"], 1)
            for i, (t0, t1) in enumerate(((0, N_CKV), (N_CKV, N_C))):
                finish_stat(dve, ST_RMS[i], 4 + i, RMS_EPS)
                for t in range(t0, t1):
                    nc.vector.tensor_tensor(craw[:, t, :], craw[:, t, :], pair(3), ALU.mult
                                            ).then_inc(S["rms_scale"], 1)
                for t in range(t0, t1):
                    gain = cc("kvg")[:, t:t + 1] if i == 0 else cc("qg")[:, t - t0:t - t0 + 1]
                    dve.wait_ge(S["rms_hi"], GROUPS * GX + t + 1)
                    nc.vector.scalar_tensor_tensor(clo[:, t, :], craw[:, t, :], gain, chi[:, t, :].bitcast(F32),
                                                   ALU.mult, ALU.subtract).then_inc(S["rms_lo"], 1)
            for i in range(N_V):
                prep_lo(dve, W_PAIR + i, (W_PAIR + i) % RAW)

        UNITS = 2 * NC_
        PAIR_BODY = 4

        def keys(i):
            t0, n = CH[i]
            return t0 + n

        def scores(u):
            at = (4 if u % 2 == 0 else 0) * BANK
            n = keys(u // 2)
            return psf[:, at:at + n] if n <= BANK else psf[:, at + LEFT:at + LEFT + n]

        def pair_pe(pe, pr, pos):
            n = W_PAIR + pr
            slot = pos % 2
            pe.wait_ge(S["w_lo"], n + 1)
            product(slot, N_CKV, chi, clo, 0, 0).then_inc(S["proj_mm"], 1)
            product(slot, N_CQ, chi, clo, N_CKV, 1, col=N_CKV * P).then_inc(S["proj_mm"], 1)
            pe.wait_ge(S["k_evac"], pr * 2 + 2)
            product(slot, N_CQ, chi, clo, N_CKV, 0, col=(N_CKV + N_CQ) * P).then_inc(S["w_used"], 1)

            def score(u):
                i, a = u // 2, u % 2
                t0, nk = CH[i][0], keys(i)
                out = scores(u)
                parts = [(0, nk)] if nk <= BANK else [(0, HALF), (HALF, nk)]
                for k0, k1 in parts:
                    mm = nc.tensor.matmul(out[:, k0:k1], qst[:, a, t0:t0 + P], kst[:, a, k0:k1],
                                          start=True, stop=i == 0, skip_group_check=True)
                if i:
                    mm = nc.tensor.matmul(out[:64, nk - 64:nk], cc("one")[0:1, :], cc("neg")[0:1, :],
                                          start=False, stop=True, skip_group_check=True)
                mm.then_inc(S["s_mm"], 1)

            pe.wait_ge(S["q_evac"], pr * 2 + 2)
            score(0)
            score(1)
            for u in range(UNITS):
                i, a = u // 2, u % 2
                x = pr * UNITS + u
                pe.wait_ge(S["s_exp"], x + 1)
                if u > 0:
                    pe.wait_ge(S["pt_first"], x)
                if u > 2:
                    pe.wait_ge(S["pt_rest"], pr * (UNITS - 2) + (u - 2))
                for j in range(i + 1):
                    k0, n2 = CH[j]
                    to = ps[:META, 7, 0:P] if j == 0 else ps[:, 6, (j - 1) * P:j * P]
                    mm = nc.tensor.transpose(to, prob[:, a, k0:k0 + n2], ident)
                mm.then_inc(S["pt_mm"], 1)
                if u + 2 < UNITS:
                    score(u + 2)
                pe.wait_ge(S["pt_first"], x + 1)
                if i:
                    pe.wait_ge(S["pt_rest"], pr * (UNITS - 2) + (u - 1))
                if u >= 2:
                    pe.wait_ge(S["pv_evac"], x - 1)
                for j in range(i + 1):
                    mm = nc.tensor.matmul(ps[:, 2 + a, 0:VH], probT[:, a, j, :],
                                          vtok[:, j, bass.ds(pr * (2 * VH) + a * VH, VH)],
                                          start=j == 0, stop=j == i)
                mm.then_inc(S["pv_mm"], 1)
            pe.wait_ge(S["pv_evac"], pr * UNITS + UNITS)
            for i in [*range(1, NC_), 0]:
                t0, n2 = CH[i]
                to = ps[:, 4, t0:t0 + n2] if i < NC_ - 1 else ps[:, 5, 0:n2]
                mm = nc.tensor.transpose(to, otok[:n2, i, :], ident[:n2, :n2])
            mm.then_inc(S["ot_mm"], 1)

        OT = [(0, CH[-1][0], 4), (CH[-1][0], T, 5)]

        def pair_act(act, pr, pos):
            act.wait_ge(S["proj_mm"], pr * 2 + 1)
            for a in range(2):
                nc.scalar.activation(kst[:NOPE, a, :], pair(0)[a * NOPE:(a + 1) * NOPE], ACT.Copy
                                     ).then_inc(S["k_evac"], 1)
            for u in range(UNITS):
                i, a = u // 2, u % 2
                x = pr * UNITS + u
                act.wait_ge(S["s_max"], x + 1)
                nc.scalar.activation(prob[:, a, :keys(i)], scores(u), ACT.Exp, bias=nmax[:, a, 0:1],
                                     accum_out=nmax[:, a, 1:2]).then_inc(S["s_exp"], 1)
                act.wait_ge(S["pt_mm"], x + 1)
                nc.scalar.activation(probT[:META, a, 0, :], ps[:META, 7, 0:P], ACT.Copy).then_inc(S["pt_first"], 1)
            prep_hi(act, W_PAIR + 2 + pr, (pos + 2) % RAW)
            act.wait_ge(S["ot_mm"], pr + 1)
            for t0, t1, b in OT:
                nc.scalar.activation(hhi[:, bass.ds(pr, 1), t0:t1], ps[:, b:b + 1, 0:t1 - t0], ACT.Copy
                                     ).then_inc(S["ot_hi"], 1)

        def pair_dve(dve, pr, pos):
            for a in range(2):
                dve.wait_ge(*((S["proj_mm"], pr * 2 + 2) if a == 0 else (S["w_used"], W_PAIR + pr + 1)))
                nc.vector.tensor_tensor(qst[:, a, :], pair(1 - a), tab[:, 0, :], ALU.mult).then_inc(S["q_evac"], 1)

            def row_max(u):
                dve.wait_ge(S["s_mm"], pr * UNITS + u + 1)
                nc.vector.tensor_reduce(nmax[:, u % 2, 0:1], scores(u), axis=AX.X, op=ALU.max, negate=True
                                        ).then_inc(S["s_max"], 1)
            row_max(0)
            row_max(1)
            for u in range(UNITS):
                i, a = u // 2, u % 2
                x = pr * UNITS + u
                dve.wait_ge(S["s_exp"], x + 1)
                nc.vector.reciprocal(nmax[:, a, 2:3], nmax[:, a, 1:2]).then_inc(S["s_rec"], 1)
                if i:
                    dve.wait_ge(S["pt_mm"], x + 1)
                    nc.vector.tensor_copy(probT[:, a, 1:i + 1, :],
                                          ps[:, 6, 0:i * P].rearrange("p (j q) -> p j q", j=i)
                                          ).then_inc(S["pt_rest"], 1)
                if u + 2 < UNITS:
                    row_max(u + 2)
                dve.wait_ge(S["pv_mm"], x + 1)
                dve.wait_ge(S["s_rec"], x + 1)
                nc.vector.tensor_scalar(otok[:, i, a * VH:(a + 1) * VH], ps[:, 2 + a, 0:VH], nmax[:, a, 2:3], None,
                                        ALU.mult).then_inc(S["pv_evac"], 1)
            prep_lo(dve, W_PAIR + 2 + pr, (pos + 2) % RAW)
            for e, (t0, t1, b) in enumerate(OT):
                dve.wait_ge(S["ot_hi"], pr * 2 + e + 1)
                nc.vector.tensor_tensor(hlo[:, bass.ds(pr, 1), t0:t1], ps[:, b:b + 1, 0:t1 - t0],
                                        hhi[:, bass.ds(pr, 1), t0:t1].bitcast(F32), ALU.subtract
                                        ).then_inc(S["ot_lo"], 1)

        def all_pairs(eng, one):
            with eng.Fori(0, N_PAIR // PAIR_BODY) as it:
                for q in range(PAIR_BODY):
                    one(eng, it * PAIR_BODY + q, (W_PAIR + q) % RAW)

        def ready(pe, name, value):
            return lambda: pe.wait_ge(S[name], value)

        @block.tensor
        def _(pe):
            ssm_pe(pe)
            out_pe(pe, W_MOUT, 2, 0, (KT, KT), ynhi, ynlo, 2, False, ready(pe, "rms_lo", GROUPS * GX))
            ln_pe(pe, 0)
            if STOP >= 2:
                ffn_pe(pe, 0, W_FIN0)
                out_pe(pe, W_FOUT0, 3, 1, fout, ahi, alo, 4, False, ready(pe, "ffn_lo", FT))
                ln_pe(pe, 1)
            if STOP >= 3:
                down_pe(pe)
                all_pairs(pe, pair_pe)
                out_pe(pe, W_O, 1, 2, (KT,), hhi, hlo, 4, False, ready(pe, "ot_lo", 2 * N_PAIR))
                ln_pe(pe, 2)
            if STOP > 3:
                ffn_pe(pe, 1, W_FIN1)
                out_pe(pe, W_FOUT1, 3, 3, fout, ahi, alo, 4, True, ready(pe, "ffn_lo", 2 * FT))
                ln_pe(pe, 3)

        @block.scalar
        def _(act):
            ssm_act(act)
            out_act(act, W_MOUT, 2, 2, False)
            ln_act(act, 0)
            if STOP >= 2:
                ffn_act(act, 0, W_FIN0)
                out_act(act, W_FOUT0, 3, 4, False)
                ln_act(act, 1)
            if STOP >= 3:
                down_act(act)
                all_pairs(act, pair_act)
                out_act(act, W_O, 1, 4, False)
                ln_act(act, 2)
            if STOP > 3:
                ffn_act(act, 1, W_FIN1)
                out_act(act, W_FOUT1, 3, 4, True)
                ln_act(act, 3)

        @block.vector
        def _(dve):
            ssm_dve(dve)
            out_dve(dve, W_MOUT, 2, 2, False)
            ln_dve(dve, 0)
            if STOP >= 2:
                ffn_dve(dve, 0, W_FIN0)
                out_dve(dve, W_FOUT0, 3, 4, False)
                ln_dve(dve, 1)
            if STOP >= 3:
                down_dve(dve)
                all_pairs(dve, pair_dve)
                out_dve(dve, W_O, 1, 4, False)
                ln_dve(dve, 2)
            if STOP > 3:
                ffn_dve(dve, 1, W_FIN1)
                out_dve(dve, W_FOUT1, 3, 4, True)
                ln_dve(dve, 3)

        @block.gpsimd
        def _(pool):
            ssm_pool(pool)
            if STOP >= 3:
                pool.wait_ge(S["w_used"], W_DOWN)
                pool.dma_start(tab[:, :, :], tabs).then_inc(S["tab_in"], 16)


def weight_tiles(w):
    k, n = w.shape
    return w.reshape(k // P, P, n // P, P).transpose(2, 1, 0, 3).reshape(n // P, P, k)


def columns(v):
    return np.moveaxis(v.reshape(v.shape[:-1] + (-1, P)), -1, 0)


def weight_stream(m_w_in, m_w_out, kv_w_down, kv_w_up, q_w_down, q_w_up, o_w, f_w_in, f_w_out):
    ssm = weight_tiles(m_w_in[0][:, :2 * INNER + 2 * GROUPS * STATE])
    z, x = ssm[:GROUPS * GX], ssm[GROUPS * GX:2 * GROUPS * GX]
    b, c = (ssm[2 * GROUPS * GX + i * GROUPS:2 * GROUPS * GX + (i + 1) * GROUPS] for i in range(2))
    parts = []
    for g in range(GROUPS):
        parts += [b[g:g + 1], c[g:g + 1], x[g * GX:(g + 1) * GX], z[g * GX:(g + 1) * GX]]
    parts.append(weight_tiles(m_w_out[0]).reshape(N_MOUT, P, WT))

    def ffn(layer):
        w = weight_tiles(f_w_in[layer])
        parts.append(np.stack([w[:FT], w[FT:]], 1).reshape(N_FIN, P, WT))
        o = np.zeros((KT, P, 3 * WT), w.dtype)
        o[:, :, :F] = weight_tiles(f_w_out[layer])
        parts.append(o.reshape(KT, P, 3, WT).transpose(0, 2, 1, 3).reshape(N_FOUT, P, WT))

    parts[-1] = weight_tiles(m_w_out[0]).reshape(KT, P, 2, WT).transpose(0, 2, 1, 3).reshape(N_MOUT, P, WT)
    ffn(0)
    pe = kv_w_down[:, KVL:]
    sw = np.concatenate([pe[:, ROPE // 2:], pe[:, :ROPE // 2]], 1)
    down = np.concatenate([kv_w_down[:, :KVL], q_w_down[0]] + [pe] * 4 + [sw] * 4, 1)
    parts.append(weight_tiles(down))
    up = kv_w_up.reshape(KVL // P, P, HEADS, NOPE + VH)
    parts.append(up[..., NOPE:].reshape(KVL // P, P, HEADS * VH))
    kn = up[..., :NOPE].reshape(KVL // P, P, HEADS // 2, 2 * NOPE)
    q = q_w_up[0].reshape(QL // P, P, HEADS, NOPE + ROPE)
    q = np.concatenate([q, q[..., NOPE + ROPE // 2:], q[..., NOPE:NOPE + ROPE // 2]], -1)
    q = q.transpose(2, 1, 0, 3).reshape(HEADS // 2, 2, P, QL // P * P)
    pairs = np.concatenate([kn.transpose(2, 1, 0, 3).reshape(HEADS // 2, P, KVL // P * P), q[:, 0], q[:, 1]], -1)
    parts.append(pairs)
    parts.append(weight_tiles(o_w[0]))
    ffn(1)
    return np.ascontiguousarray(np.concatenate(parts, 0))


def constants(m_w_in, m_conv_w, m_conv_b, m_dt_bias, m_a_log, m_d, m_norm_g, kv_norm_g, q_norm_g,
              f_conv_w, f_conv_b, ln_g, ln_b):
    f = np.float32
    out = np.zeros((P, NCON), f)

    def put(name, v):
        out[:, CC[name][0]:CC[name][1]] = v.reshape(P, -1)
    r = np.arange(P)
    put("ident", np.eye(P, dtype=f))
    put("triu", (r[:, None] <= r[None, :]).astype(f))
    put("strict", (r[:, None] > r[None, :]).astype(f))
    put("wdt", m_w_in[0][:, 2 * INNER + 2 * GROUPS * STATE:].reshape(KT, P, SSM_HEADS).transpose(1, 0, 2))
    put("dtb", np.broadcast_to(m_dt_bias[0], (P, SSM_HEADS)))
    put("alog", np.broadcast_to(m_a_log[0], (P, SSM_HEADS)))
    cw, cb = columns(m_conv_w[0]), columns(m_conv_b[0])
    w, b = np.zeros((P, N_SSM, TAPS), f), np.zeros((P, N_SSM), f)
    for g in range(GROUPS):
        src = [GROUPS * GX + g, GROUPS * GX + GROUPS + g] + [g * GX + j for j in range(GX)]
        for j, t in enumerate(src):
            w[:, g * GT + j, :] = cw[:, :, t]
            b[:, g * GT + j] = cb[:, t]
    put("cw", w)
    put("cb", b)
    put("dsk", columns(np.repeat(m_d[0], HD)))
    put("ng", columns(m_norm_g[0]))
    fw = columns(f_conv_w).reshape(P, 2, FTAPS, 2, FT)
    put("fw", fw.transpose(0, 1, 4, 3, 2))
    put("fb", columns(f_conv_b).reshape(P, 2, 2, FT).transpose(0, 1, 3, 2))
    put("lng", columns(ln_g))
    put("lnb", columns(ln_b))
    put("kvg", columns(kv_norm_g))
    put("qg", columns(q_norm_g[0]))
    out[0, CC["neg"][0]:CC["neg"][1]] = -1e30
    out[0, CC["one"][0]:CC["one"][1]] = 1.0
    return out


def rotary_tables():
    half = ROPE // 2
    inv = np.float32(10000.0) ** (-np.arange(half, dtype=np.float32) * np.float32(2.0) / np.float32(ROPE))
    ang = (inv[:, None] * np.arange(T, dtype=np.float32)[None, :]).astype(np.float64)
    cos = np.concatenate([np.cos(ang)] * 2, 0)
    sin = np.concatenate([-np.sin(ang), np.sin(ang)], 0)
    q = np.concatenate([np.ones((NOPE, T)), cos, sin], 0) * SC
    return np.stack([q, np.concatenate([cos] * 4, 0), np.concatenate([sin] * 4, 0)], 1).astype(np.float32)


STOP_AT = None


def kernel(x, meta_tokens, m_w_in, m_conv_w, m_conv_b, m_dt_bias, m_a_log, m_d, m_norm_g, m_w_out,
           kv_w_down, kv_norm_g, kv_w_up, q_w_down, q_norm_g, q_w_up, o_w, f_w_in, f_conv_w, f_conv_b,
           f_w_out, ln_g, ln_b):
    import concourse.bacc as bacc
    from concourse.bass_utils import run_bass_kernel_spmd

    a = {k: np.asarray(v) for k, v in locals().items() if isinstance(v, np.ndarray) or hasattr(v, "shape")}
    (x, meta_tokens, m_w_in, m_conv_w, m_conv_b, m_dt_bias, m_a_log, m_d, m_norm_g, m_w_out, kv_w_down,
     kv_norm_g, kv_w_up, q_w_down, q_norm_g, q_w_up, o_w, f_w_in, f_conv_w, f_conv_b, f_w_out, ln_g,
     ln_b) = a.values()
    tokens = np.concatenate([meta_tokens, x[0]], 0)
    arrays = {
        "wstream": weight_stream(m_w_in, m_w_out, kv_w_down, kv_w_up, q_w_down, q_w_up, o_w, f_w_in, f_w_out),
        "xT": np.ascontiguousarray(tokens.reshape(T, KT, P).transpose(2, 1, 0)),
        "consts": constants(m_w_in, m_conv_w, m_conv_b, m_dt_bias, m_a_log, m_d, m_norm_g, kv_norm_g,
                            q_norm_g, f_conv_w, f_conv_b, ln_g, ln_b),
        "tabs": rotary_tables(),
    }
    nc = bacc.Bacc("TRN2", target_bir_lowering=False, num_devices=1)
    aps = [nc.dram_tensor(n, v.shape, F32, kind="ExternalInput").ap() for n, v in arrays.items()]
    out = nc.dram_tensor("outT", (P, KT, SEQ), F32, kind="ExternalOutput").ap()
    build(nc, *aps, out, STOP_AT)
    got = run_bass_kernel_spmd(nc, [arrays], core_ids=[0]).results[0]["outT"]
    return np.ascontiguousarray(got.transpose(2, 1, 0).reshape(1, SEQ, D))
```

```python
from contextlib import ExitStack

import numpy as np
import concourse.bass as bass
from concourse import mybir

F32 = mybir.dt.float32
F32R = mybir.dt.float32r
ACT = mybir.ActivationFunctionType
ALU = mybir.AluOpType
AX = mybir.AxisListType

P = 128
D = 1024
SEQ = 512
META = 16
T = META + SEQ
HALF = T // 2
BANK = 512
LEFT = BANK - HALF
KT = D // P
ALPHA = float((2.0 * 2) ** 0.25)
LN_EPS = 1e-5
RMS_EPS = 1e-6

CH = [(0, META)] + [(META + P * i, P) for i in range(SEQ // P)]
NC_ = len(CH)
KEY_TILES = -(-T // P)

SSM_HEADS, HD, GROUPS, STATE = 32, 64, 4, 128
INNER = SSM_HEADS * HD
GH = SSM_HEADS // GROUPS
GX = INNER // GROUPS // P
GT = 2 + 2 * GX
TAPS, FTAPS = 4, 3

HEADS, NOPE, ROPE, VH = 16, 64, 32, 64
QL, KVL = 384, 256
F = 2816
FT = F // P
SC = float(NOPE + ROPE) ** -0.5


N_SSM = GROUPS * GT
N_MOUT = KT * (INNER // D)
N_FIN = 2 * FT
N_FOUT = KT * 3
N_DOWN = 7
N_V = 2
N_PAIR = HEADS // 2
N_O = KT
W_SSM = 0
W_MOUT = W_SSM + N_SSM
W_FIN0 = W_MOUT + N_MOUT
W_FOUT0 = W_FIN0 + N_FIN
W_DOWN = W_FOUT0 + N_FOUT
W_V = W_DOWN + N_DOWN
W_PAIR = W_V + N_V
W_O = W_PAIR + N_PAIR
W_FIN1 = W_O + N_O
W_FOUT1 = W_FIN1 + N_FIN
NW = W_FOUT1 + N_FOUT
ST_OF_LN = (GROUPS, GROUPS + 1, GROUPS + 4, GROUPS + 5)
ST_RMS = (GROUPS + 2, GROUPS + 3)
MIX_ORDER = ((0, 0), (1, 0), (0, 1), (1, 1)) + tuple((m, s) for m in range(2, KT) for s in range(2))
ST = 88
NS = T // ST
assert NS * ST == T and HALF % ST == 0
MEAN_OF = (D, INNER // GROUPS, KVL, QL)
RAW = 4
WT = KT * P


def const_columns():
    at, out = 0, {}
    for name, n in (("ident", P), ("triu", P), ("strict", P), ("wdt", KT * SSM_HEADS),
                    ("dtb", SSM_HEADS), ("alog", SSM_HEADS), ("cw", (N_SSM) * TAPS), ("cb", N_SSM),
                    ("dsk", GROUPS * GX), ("ng", GROUPS * GX), ("fw", 2 * N_FIN * FTAPS),
                    ("fb", 2 * N_FIN), ("lng", 4 * KT), ("lnb", 4 * KT), ("kvg", 2), ("qg", 3),
                    ("neg", 64), ("one", 64)):
        out[name] = (at, at + n)
        at += n
    return out, at


CC, NCON = const_columns()


def build(nc, wstream, xT, consts, tabs, outT, stop=None):
    ctx = ExitStack()
    with ctx:
        def sb(name, shape, dt=F32, c=ctx):
            return c.enter_context(nc.sbuf_tensor(name, shape, dt))

        def sem(name):
            return ctx.enter_context(nc.semaphore(name))

        h = sb("h", [P, KT, T])
        hhi = sb("hhi", [P, KT, T], F32R)
        hlo = sb("hlo", [P, KT, T], F32R)
        raw = sb("raw", [P, RAW, WT])
        whi = sb("whi", [P, 2, WT], F32R)
        wlo = sb("wlo", [P, 2, WT], F32R)
        tmp = sb("tmp", [P, 4, T])
        con = sb("con", [P, NCON])
        mean_mat = sb("mean_mat", [P, P])
        pick = sb("pick", [P, len(MEAN_OF), NS, NS])
        eps = sb("eps", [P, 2])
        dev = sb("dev", [NS, 2, ST])
        ones = sb("ones", [P, P])

        inv = tmp[:NS, 1, :]

        def cc(name):
            return con[:, CC[name][0]:CC[name][1]]
        ident, triu, strict = cc("ident"), cc("triu"), cc("strict")
        wdt = cc("wdt").rearrange("p (k n) -> p k n", k=KT)
        cw = cc("cw").rearrange("p (t n) -> p t n", t=N_SSM)
        fw = cc("fw").rearrange("p (t n) -> p t n", t=2 * N_FIN)
        cb, fb, dsk, ng, lng, lnb = (cc(n) for n in ("cb", "fb", "dsk", "ng", "lng", "lnb"))

        ssm = ExitStack()
        ynhi = sb("ynhi", [P, GROUPS * GX, T], F32R, ssm)
        ynlo = sb("ynlo", [P, GROUPS * GX, T], F32R, ssm)
        xy = sb("xy", [P, 2, GX, T], F32, ssm)
        bT = sb("bT", [P, T], F32, ssm)
        cT = sb("cT", [P, T], F32, ssm)
        sdec = sb("sdec", [P, GH * HD], F32, ssm)
        decay_rhs = sb("decay_rhs", [P, 2, GH * P], F32R, ssm)
        a_parts = sb("a_parts", [P, 2, NC_, SSM_HEADS], F32R, ssm)
        strict_r = sb("strict_r", [P, P], F32R, ssm)
        btok = sb("btok", [P, P], F32, ssm)
        cbm = sb("cbm", [P, P], F32, ssm)
        xdt = sb("xdt", [P, GH * HD], F32, ssm)
        xw = sb("xw", [P, GH * HD], F32, ssm)
        ytok = sb("ytok", [P, GH * HD], F32, ssm)
        state = sb("state", [P, GH * HD], F32, ssm)
        dtt = sb("dtt", [P, 4, NC_, SSM_HEADS], F32, ssm)
        ssm.close()
        hflat = h[:, :, :].rearrange("p k t -> p (k t)")
        decay = [hflat[:META, 4 * GH * P:4 * GH * P + GH * META].rearrange("p (a l) -> p a l", a=GH)] + [
            hflat[:, i * GH * P:(i + 1) * GH * P].rearrange("p (a l) -> p a l", a=GH) for i in range(4)]
        dt_, acs_, suf_, tot_ = (dtt[:, i] for i in range(4))
        e_ = tmp[:, 0, 0:NC_ * SSM_HEADS].rearrange("p (c n) -> p c n", c=NC_)
        negA = tmp[:, 1, 0:SSM_HEADS]
        a_ = tmp[:, 2, 0:NC_ * SSM_HEADS].rearrange("p (c n) -> p c n", c=NC_)

        ffn = ExitStack()
        ahi = sb("ahi", [P, FT, T], F32R, ffn)
        alo = sb("alo", [P, FT, T], F32R, ffn)
        ffn.close()

        lns = ExitStack()
        ln_squares = sb("ln_squares", [P, KT, T], F32, lns)
        lns.close()

        att = ExitStack()
        vtok = sb("vtok", [P, KEY_TILES, HEADS * VH], F32, att)
        chi = sb("chi", [P, 5, T], F32R, att)
        clo = sb("clo", [P, 5, T], F32R, att)
        craw = sb("craw", [P, 5, T], F32, att)
        tab = sb("tab", [P, 3, T], F32, att)
        kst = sb("kst", [P, 2, 2, T], F32, att)
        qst = sb("qst", [P, 2, 2, T], F32, att)
        prob = [sb(f"prob{i}", [P, 2, (i + 1) * P], F32, att) for i in range(NC_)]
        probT = sb("probT", [P, 2, KEY_TILES, P], F32, att)
        otok = sb("otok", [P, 2, NC_, P], F32, att)
        nmax = sb("nmax", [P, 4, 3], F32, att)
        att.close()

        ps = ctx.enter_context(nc.psum_tensor("ps", [P, 8, BANK], F32))
        psf = ps[:, :, :].rearrange("p b n -> p (b n)")

        def pair(i, half=None, t0=0):
            n = (T - t0) // 2
            at = 2 * i * BANK + BANK - n
            return psf[:, at:at + 2 * n] if half is None else psf[:, at + n * half:at + n * (half + 1)]

        names = """att_zero const_in tab_in out_done set_up
            w_hi w_lo w_used
            h_hi0 h_lo0
            dt_mm dt_bias dt_act dt_dve dt_cs dt_exp
            rhs_built decay_mm decay_exp
            conv_first conv_taps conv_silu z_silu
            ssd_in btok_ready xw_ready ssd_local ssd_state ssd_yoff ssd_out ytok_ready state_ready ssd_back y_ready
            gate_mul gate_sq
            st_mm st_sqrt st_inv st_rec st_bc h_sum sq_sum mean_mm
            proj_mm conv_tap dt_split yoff state_decay ln_center ln_sq ln_scale ln_hi_act ln_hi_dve ln_h ln_lo_pool ln_lo_dve
            rms_scale rms_hi rms_lo
            h_back out_evac
            ffn_first ffn_silu ffn_mul ffn_hi ffn_lo
            down_copy down_sq kpe v_mm v_evac
            k_evac q_evac s_mm s_max s_exp s_rec pt_mm pt_act pt_dve pv_mm pv_evac ot_mm ot_hi ot_lo""".split()
        S = {n: sem(n) for n in names}
        x_in = [sem(f"x_in{i}") for i in range(KT // 2)]
        load = [sem(f"w_load{i}") for i in range(RAW)]
        block = ctx.enter_context(nc.Block())
        STOP = {None: 9, "ssm": 1, "l0": 2, "attn": 3}[stop]
        end = {9: NW, 1: W_FIN0 + 2, 2: W_DOWN + 2, 3: W_FIN1 + 2}[STOP]
        LNH_END = KT * min(STOP, 4)

        @block.sync
        def _(sp):
            def fetch(n, q):
                sp.dma_start(raw[:, n % RAW if isinstance(n, int) else q, :],
                             wstream[bass.ds(n, 1)].rearrange("a p n -> p (a n)") if not isinstance(n, int)
                             else wstream[n]).then_inc(load[q], 16)

            for k in range(0, KT, 2):
                sp.dma_start(h[:, k:k + 2, :], xT[:, k:k + 2, :]).then_inc(x_in[k // 2], 16)
                if k == 0:
                    fetch(0, 0)
            sp.dma_start(con[:, :], consts).then_inc(S["const_in"], 16)
            for n in range(1, RAW):
                fetch(n, n % RAW)
            full = end // RAW
            with sp.Fori(1, full) as g:
                for q in range(RAW):
                    sp.wait_ge(S["w_lo"], g * RAW + (q - RAW + 1))
                    fetch(g * RAW + q, q)
            for n in range(full * RAW, end):
                sp.wait_ge(S["w_lo"], n - RAW + 1)
                fetch(n, n % RAW)
            for k in range(0, KT, 2):
                sp.wait_ge(S["ln_h"], LNH_END - KT + k + 2)
                sp.dma_start(outT[:, k:k + 2, :], h[:, k:k + 2, META:T]).then_inc(S["out_done"], 16)
            sp.wait_ge(S["out_done"], 16 * (KT // 2))

        def prep_hi(act, n, q):
            act.wait_ge(load[q], (n - q) * (16 // RAW) + 16)
            if not (isinstance(n, int) and n < 2):
                act.wait_ge(S["w_used"], n - 1)
            nc.scalar.activation(whi[:, q % 2, :], raw[:, q, :], ACT.Copy).then_inc(S["w_hi"], 1)

        def prep_lo(dve, n, q):
            dve.wait_ge(S["w_hi"], n + 1)
            nc.vector.tensor_tensor(wlo[:, q % 2, :], raw[:, q, :], whi[:, q % 2, :].bitcast(F32),
                                    ALU.subtract).then_inc(S["w_lo"], 1)

        def product(slot, nk, xhi, xlo, k0, bank_pair, first=True, last=True, before_k=None, col=0, part=(0, 1),
                    t0=0):
            nt = (T - t0) // 2
            ks = range(nk * part[0] // part[1], nk * (part[0] + 1) // part[1])
            for k in ks:
                if before_k is not None:
                    before_k(k)
                for p, (w, x) in enumerate(((whi, xhi), (whi, xlo), (wlo, xhi))):
                    for half in range(2):
                        mm = nc.tensor.matmul(pair(bank_pair, half, t0), w[:, slot, col + k * P:col + (k + 1) * P],
                                              x[:, k0 + k, t0 + nt * half:t0 + nt * (half + 1)],
                                              start=first and k == 0 and p == 0,
                                              stop=last and k == nk - 1 and p == 2, skip_group_check=True)
            return mm

        def stats_mm(pe, tiles, which, bank_pair, waits):
            for k, src in enumerate(tiles):
                waits(k)
                for c in range(NS):
                    mm = nc.tensor.matmul(ps[:NS, 2 * bank_pair, 0:ST], pick[:, which, c, :],
                                          src[:, c * ST:(c + 1) * ST], start=k == 0 and c == 0,
                                          stop=k == len(tiles) - 1 and c == NS - 1, skip_group_check=True)
            return mm

        def stat_sqrt(act, n, bank_pair, which_eps):
            act.wait_ge(S["st_mm"], n + 1)
            nc.scalar.activation(dev[:, 0, :], ps[:NS, 2 * bank_pair, 0:ST], ACT.Sqrt,
                                 bias=eps[:NS, which_eps:which_eps + 1]).then_inc(S["st_sqrt"], 1)

        def stat_rec(dve, n):
            dve.wait_ge(S["st_sqrt"], n + 1)
            nc.vector.reciprocal(dev[:, 1, :], dev[:, 0, :]).then_inc(S["st_inv"], 1)
            dve.wait_ge(S["st_inv"], n + 1)
            nc.vector.tensor_tensor(inv.rearrange("p (c i) -> p c i", c=NS),
                                    dev[:, 1, :].unsqueeze(1).broadcast_to([NS, NS, ST]),
                                    ident[:NS, :NS].unsqueeze(2).broadcast_to([NS, NS, ST]), ALU.mult
                                    ).then_inc(S["st_rec"], 1)

        def stat_spread(pe, n, bank_pair):
            pe.wait_ge(S["st_rec"], n + 1)
            for half in range(2):
                mm = nc.tensor.matmul(pair(bank_pair, half), ones[:NS, :], inv[:, HALF * half:HALF * (half + 1)],
                                      start=True, stop=True)
            mm.then_inc(S["st_bc"], 1)

        h_sum = tmp[:, 3, :]
        OUT_BODY = KT // 2

        def h_sum_pool(pool, L):
            for k in range(1, KT - 1):
                pool.wait_ge(S["out_evac"], 2 + KT * L + k + 1)
                if k > 1:
                    pool.wait_ge(S["h_sum"], (KT - 2) * L + k - 1)
                nc.gpsimd.tensor_tensor(h_sum, h[:, 0, :] if k == 1 else h_sum, h[:, k, :], ALU.add
                                        ).then_inc(S["h_sum"], 1)

        def ln_pe(pe, L):
            for tile, name, value in ((h_sum, "h_sum", (KT - 2) * (L + 1)), (h[:, KT - 1, :], "out_evac", 2 + KT * (L + 1))):
                pe.wait_ge(S[name], value)
                for half in range(2):
                    mm = nc.tensor.matmul(pair(3, half), mean_mat[:, :], tile[:, HALF * half:HALF * (half + 1)],
                                          start=name == "h_sum", stop=name == "out_evac", skip_group_check=True)
            mm.then_inc(S["mean_mm"], 1)
            stats_mm(pe, [square_of(k) for k in range(KT)], 0, 2,
                     lambda k: pe.wait_ge(S["ln_sq"], KT * L + k + 1)).then_inc(S["st_mm"], 1)
            stat_spread(pe, ST_OF_LN[L], 2)

        def square_of(k):
            return ln_squares[:, k, :]

        def ln_act(act, L):
            for k in range(KT):
                act.wait_ge(S["ln_center"], KT * L + k + 1)
                nc.scalar.activation(square_of(k), h[:, k, :], ACT.Square).then_inc(S["ln_sq"], 1)
            stat_sqrt(act, ST_OF_LN[L], 2, 0)
            for k in range(KT):
                j = L * KT + k
                act.wait_ge(S["ln_scale"], j + 1)
                nc.scalar.activation(h[:, k, :], h[:, k, :], ACT.Identity, bias=lnb[:, j:j + 1],
                                     scale=lng[:, j:j + 1]).then_inc(S["ln_h"], 1)
                if L < 3 and k % 2:
                    act.wait_ge(S["ln_h"], j + 1)
                    nc.scalar.activation(hhi[:, k, :], h[:, k, :], ACT.Copy).then_inc(S["ln_hi_act"], 1)

        def ln_dve(dve, L):
            dve.wait_ge(S["mean_mm"], L + 1)
            for k in range(KT):
                nc.vector.tensor_tensor(h[:, k, :], h[:, k, :], pair(3), ALU.subtract).then_inc(S["ln_center"], 1)
            stat_rec(dve, ST_OF_LN[L])
            dve.wait_ge(S["ln_sq"], KT * L + KT)
            dve.wait_ge(S["st_bc"], ST_OF_LN[L] + 1)

            def split(k):
                if L < 3 and k % 2 == 0:
                    dve.wait_ge(S["ln_h"], KT * L + k + 1)
                    nc.vector.tensor_copy(hhi[:, k, :], h[:, k, :]).then_inc(S["ln_hi_dve"], 1)
                    dve.wait_ge(S["ln_hi_dve"], (KT * L + k) // 2 + 1)
                    nc.vector.tensor_tensor(hlo[:, k, :], h[:, k, :], hhi[:, k, :].bitcast(F32), ALU.subtract
                                            ).then_inc(S["ln_lo_dve"], 1)

            for k in range(KT):
                nc.vector.tensor_tensor(h[:, k, :], h[:, k, :], pair(2), ALU.mult).then_inc(S["ln_scale"], 1)
                if k > 0:
                    split(k - 1)
            split(KT - 1)

        def ln_pool(pool, L):
            for k in range(1, KT, 2):
                pool.wait_ge(S["ln_hi_act"], (KT * L + k) // 2 + 1)
                nc.gpsimd.tensor_tensor(hlo[:, k, :], h[:, k, :], hhi[:, k, :].bitcast(F32),
                                        ALU.subtract).then_inc(S["ln_lo_pool"], 1)

        def stream_ready(pe, L, k):
            pe.wait_ge(S["ln_lo_pool"] if k % 2 else S["ln_lo_dve"], (KT * L + k) // 2 + 1)

        NX = 2 + GX
        IN_PE = (("z", 0, 0), ("z", 0, 1), ("in", 0), ("z", 1, 0), ("out", 0), ("in", 1), ("z", 1, 1),
                 ("back", 0), ("out", 1), ("in", 2), ("z", 2, 0), ("back", 1), ("out", 2), ("in", 3),
                 ("z", 2, 1), ("back", 2), ("out", 3), ("in", 4), ("z", 3, 0), ("back", 3), ("out", 4),
                 ("z", 3, 1), ("back", 4))
        IN_DVE = (("in", 0), ("z", 0), ("out", 0), ("in", 1), ("out", 1), ("in", 2), ("back", 0), ("z", 1),
                  ("out", 2), ("in", 3), ("back", 1), ("out", 3), ("in", 4), ("back", 2), ("z", 2),
                  ("out", 4), ("back", 3), ("back", 4), ("z", 3))
        IN_ACT = (("z", 0), ("in", 0), ("in", 1), ("z", 1), ("in", 2), ("in", 3), ("z", 2), ("in", 4), ("z", 3))

        def decays_before(g, j):
            first = 2 if g == 0 else 0
            return (j - first,) if 0 <= j - first < NC_ else ()

        def ssm_pe(pe):
            for g in range(GROUPS):
                ssm_group_pe(pe, g)

        def dt_pe(pe):
            pe.wait_ge(S["const_in"], 16)
            for c, (t0, n) in enumerate(CH):
                for k in range(KT):
                    mm = nc.tensor.matmul(ps[:n, 4, c * SSM_HEADS:(c + 1) * SSM_HEADS], h[:, k, t0:t0 + n],
                                          wdt[:, k, :], start=k == 0, stop=k == KT - 1)
            mm.then_inc(S["dt_mm"], 1)

        def dt_sums_pe(pe):
            pe.wait_ge(S["dt_dve"], DT_STEPS)
            pe.wait_ge(S["set_up"], SET_UP)
            for b, left in ((5, triu), (6, strict), (7, ones)):
                m0 = P if b == 7 else META
                nc.tensor.matmul(ps[:m0, b, 0:SSM_HEADS], left[:META, :m0], a_[:META, 0, :], start=True, stop=True)
                mm = nc.tensor.matmul(ps[:, b, SSM_HEADS:NC_ * SSM_HEADS], left[:, :], a_[:, 1:, :],
                                      start=True, stop=True)
                mm.then_inc(S["dt_cs"] if b == 5 else S["decay_mm"], 1)

        def decay_pe(pe, g, c):
            u, n = g * NC_ + c, CH[c][1]
            pe.wait_ge(S["rhs_built"], u + 1)
            if u == 1:
                pe.wait_ge(S["dt_exp"], 5)
            if c >= 2:
                pe.wait_ge(S["decay_exp"], u - 1)
            b = 4 + 2 * (c % 2)
            for at in range(0, GH * n, BANK):
                to = min(at + BANK, GH * n)
                for part in range(2):
                    mm = nc.tensor.matmul(ps[:, b + at // BANK, 0:to - at], strict_r[:n, :],
                                          decay_rhs[:n, part, at:to], start=part == 0, stop=part == 1)
            mm.then_inc(S["decay_mm"], 1)

        def ssm_group_pe(pe, g):
            q = g % 2
            for j in range(NX):
                n = g * GT + j
                for c in decays_before(g, j):
                    decay_pe(pe, g, c)
                pe.wait_ge(S["w_lo"], n + 1)
                if j >= 2:
                    pe.wait_ge(S["conv_taps"], g * NX + (j - 1))
                elif g > 0 and j == 0:
                    pe.wait_ge(S["z_silu"], g * GX)
                elif g > 0 and j == 1:
                    pe.wait_ge(S["y_ready"], g * (NC_ * GX))
                product(n % 2, KT, hhi, hlo, 0, j % 2,
                        before_k=(lambda k: pe.wait_ge(S["h_lo0"], k + 1)) if n == 0 else None
                        ).then_inc(S["w_used"], 1)
                if n == 0:
                    dt_pe(pe)
                if n == 1:
                    dt_sums_pe(pe)
                if g > 0 and j == 3:
                    pe.wait_ge(S["decay_exp"], g * NC_ + NC_ - 1)
                    norm_pe_sum(pe, g - 1)
                if g > 0 and j == 4:
                    stat_spread(pe, g - 1, 3)
            for kind, c, *half in IN_PE:
                u = g * NC_ + c
                if kind == "z":
                    n = g * GT + NX + c
                    if half[0] == 0:
                        pe.wait_ge(S["w_lo"], n + 1)
                        if c == 0:
                            pe.wait_ge(S["conv_taps"], g * NX + NX - 1)
                        else:
                            pe.wait_ge(S["z_silu"], g * GX + c)
                    if half[0] and c == 0:
                        for late in decays_before(g, NX):
                            decay_pe(pe, g, late)
                    mm = product(n % 2, KT, hhi, hlo, 0, 0, part=(half[0], 2))
                    if half[0]:
                        mm.then_inc(S["w_used"], 1)
                    continue
                t0, n = CH[c]
                if kind == "in":
                    if c == 0:
                        pe.wait_ge(S["conv_silu"], (g + 1) * NX)
                        pe.wait_ge(S["decay_exp"], u + NC_)
                    for j in range(GX):
                        nc.tensor.transpose(ps[:n, 4, j * P:(j + 1) * P], xy[:, q, j, t0:t0 + n], ident)
                    nc.tensor.transpose(ps[:n, 5, 0:P], bT[:, t0:t0 + n], ident)
                    nc.tensor.matmul(ps[:n, 5, P:P + n], bT[:, t0:t0 + n], cT[:, t0:t0 + n],
                                     start=True, stop=True).then_inc(S["ssd_in"], 1)
                elif kind == "out":
                    pe.wait_ge(S["ssd_local"], u * 3 + 3)
                    pe.wait_ge(S["btok_ready"], u + 1)
                    if c < NC_ - 1:
                        pe.wait_ge(S["xw_ready"], g * (NC_ - 1) + c + 1)
                    if c == 0 and g > 0:
                        pe.wait_ge(S["rms_scale"], g * GX)
                    if c > 0:
                        pe.wait_ge(S["ytok_ready"], u)
                        pe.wait_ge(S["state_ready"], g * (NC_ - 1) + c)
                    if c < NC_ - 1:
                        nc.tensor.matmul(ps[:, 2, :], btok[:n, :], xw[:n, :], start=True, stop=True
                                         ).then_inc(S["ssd_state"], 1)
                    if c > 0:
                        nc.tensor.matmul(ps[:n, 7, :], cT[:, t0:t0 + n], state[:, :], start=True, stop=True
                                         ).then_inc(S["ssd_yoff"], 1)
                    for a in range(GH):
                        mm = nc.tensor.matmul(ps[:n, 6, a * HD:(a + 1) * HD], decay[c][:n, a, :n],
                                              xdt[:n, a * HD:(a + 1) * HD], start=True, stop=True)
                    mm.then_inc(S["ssd_out"], 1)
                else:
                    pe.wait_ge(S["ytok_ready"], u + 1)
                    if c > 0:
                        pe.wait_ge(S["y_ready"], u * GX)
                    for j in range(GX):
                        mm = nc.tensor.transpose(ps[:, 3, j * P:(j + 1) * P], ytok[:, j * P:(j + 1) * P], ident)
                    mm.then_inc(S["ssd_back"], 1)

        def norm_pe_sum(pe, g):
            stats_mm(pe, [tmp[:, 0, :]], 1, 3, lambda j: pe.wait_ge(S["sq_sum"], (g + 1) * (GX - 1))
                     ).then_inc(S["st_mm"], 1)

        DT_STEPS = 8
        SET_UP = 3 + len(MEAN_OF) + 2 + 3

        def ssm_act(act):
            for k in range(KT):
                act.wait_ge(x_in[k // 2], 16)
                nc.scalar.activation(hhi[:, k, :], h[:, k, :], ACT.Copy).then_inc(S["h_hi0"], 1)
                if k == 1:
                    prep_hi(act, 0, 0)
            prep_hi(act, 1, 1)
            act.wait_ge(S["const_in"], 16)
            act.wait_ge(S["set_up"], SET_UP)
            act.wait_ge(S["dt_bias"], 2)
            nc.scalar.activation(e_, dt_, ACT.Abs).then_inc(S["dt_act"], 1)
            act.wait_ge(S["dt_act"], 1)
            nc.scalar.activation(e_, e_, ACT.Exp, scale=-1.0).then_inc(S["dt_act"], 1)
            nc.scalar.activation(negA, cc("alog"), ACT.Exp).then_inc(S["dt_act"], 1)
            act.wait_ge(S["dt_dve"], 1)
            nc.scalar.activation(suf_, tot_, ACT.Ln).then_inc(S["dt_act"], 1)
            for g in range(GROUPS):
                ssm_group_act(act, g)

        def dt_sums_act(act):
            act.wait_ge(S["decay_mm"], 2)
            act.wait_ge(S["dt_cs"], 1)
            acs_ps = ps[:, 5, 0:NC_ * SSM_HEADS].rearrange("p (c n) -> p c n", c=NC_)
            suf_ps = ps[:, 6, 0:NC_ * SSM_HEADS].rearrange("p (c n) -> p c n", c=NC_)
            tot_ps = ps[:, 7, 0:NC_ * SSM_HEADS].rearrange("p (c n) -> p c n", c=NC_)
            for to, frm in ((acs_[:META, 0], acs_ps[:META, 0]), (acs_[:, 1:], acs_ps[:, 1:]),
                            (suf_[:META, 0], suf_ps[:META, 0]), (suf_[:, 1:], suf_ps[:, 1:]), (tot_, tot_ps)):
                nc.scalar.activation(to, frm, ACT.Exp).then_inc(S["dt_exp"], 1)
            act.wait_ge(S["h_lo0"], KT)

        def ssm_group_act(act, g):
            q = g % 2
            dst = [bT[:, :], cT[:, :]] + [xy[:, q, j, :] for j in range(GX)]
            flush = NX - 2 if g == 0 else NC_ - 1

            def silu(j):
                act.wait_ge(S["conv_taps"], g * NX + j + 1)
                nc.scalar.activation(dst[j], dst[j], ACT.Silu).then_inc(S["conv_silu"], 1)

            def decay_exp(c):
                act.wait_ge(S["decay_mm"], g * NC_ + c + 3)
                nt, b = CH[c][1], 4 + 2 * (c % 2)
                src = ps[:nt, b, 0:GH * nt] if c == 0 else psf[:, b * BANK:(b + 2) * BANK]
                nc.scalar.activation(decay[c], src.rearrange("p (a l) -> p a l", a=GH), ACT.Exp
                                     ).then_inc(S["decay_exp"], 1)

            for j in range(NX):
                n = g * GT + j
                if n == 2:
                    dt_sums_act(act)
                for c in decays_before(g, j):
                    decay_exp(c)
                act.wait_ge(S["w_used"], n + 1)
                nc.scalar.activation(dst[j], pair(j % 2), ACT.Identity, bias=cb[:, n:n + 1],
                                     scale=cw[:, n:n + 1, TAPS - 1]).then_inc(S["conv_first"], 1)
                prep_hi(act, n + 2, (n + 2) % RAW)
                if g > 0 and j == 0:
                    norm_act_sq(act, g - 1, 1 - q)
                if j == flush:
                    for jj in range(flush):
                        silu(jj)
                elif j > flush and g > 0:
                    silu(j - 1)
                if g > 0 and j == 3:
                    stat_sqrt(act, g - 1, 3, 1)
                if g > 0 and j == 5:
                    norm_act_hi(act, g - 1, 1 - q)
            for c in decays_before(g, NX):
                decay_exp(c)
            for j in range(flush if g == 0 else NX - 1, NX):
                silu(j)
            for kind, c in IN_ACT:
                if kind == "z":
                    n = g * GT + NX + c
                    act.wait_ge(S["w_used"], n + 1)
                    nc.scalar.activation(tmp[:, c, :], pair(0), ACT.Silu).then_inc(S["z_silu"], 1)
                    prep_hi(act, n + 2, (n + 2) % RAW)
                else:
                    act.wait_ge(S["ssd_in"], g * NC_ + c + 1)
                    nc.scalar.activation(btok[:CH[c][1], :], ps[:CH[c][1], 5, 0:P], ACT.Copy
                                         ).then_inc(S["btok_ready"], 1)

        def norm_act_sq(act, g, q):
            for j in range(GX):
                act.wait_ge(S["gate_mul"], g * GX + j + 1)
                nc.scalar.activation(tmp[:, j, :], xy[:, q, j, :], ACT.Square).then_inc(S["gate_sq"], 1)

        def norm_act_hi(act, g, q):
            for j in range(GX):
                act.wait_ge(S["rms_scale"], g * GX + j + 1)
                nc.scalar.activation(ynhi[:, g * GX + j, :], xy[:, q, j, :], ACT.Copy,
                                     scale=ng[:, g * GX + j:g * GX + j + 1]).then_inc(S["rms_hi"], 1)

        def ssm_pool(pool):
            pool.wait_ge(S["const_in"], 16)
            pool.wait_ge(S["dt_dve"], DT_STEPS)
            def rhs(g, c):
                if g == GROUPS:
                    return
                u, n = g * NC_ + c, CH[c][1]
                if u > 0:
                    pool.wait_ge(S["decay_mm"], u + 2)
                for part in range(2):
                    out = decay_rhs[:n, part, 0:GH * n].rearrange("p (a l) -> p a l", a=GH)
                    op = nc.gpsimd.tensor_tensor(
                        out, a_parts[:n, part, c, g * GH:(g + 1) * GH].bitcast(F32).unsqueeze(2).broadcast_to([n, GH, n]),
                        triu[:n, :n].unsqueeze(1).broadcast_to([n, GH, n]), ALU.mult)
                op.then_inc(S["rhs_built"], 1)

            rhs(0, 0)
            for g in range(GROUPS):
                for c in range(1, NC_):
                    rhs(g, c)
                    if g > 0:
                        for j in {2: (1,), 3: (2, 3)}.get(c, ()):
                            square_sum(pool, g - 1, j)
                for c in range(NC_ - 1):
                    n, gh = CH[c][1], slice(g * GH, (g + 1) * GH)
                    pool.wait_ge(S["ssd_local"], (g * NC_ + c) * 3 + 1)
                    pool.wait_ge(S["dt_exp"], 5)
                    nc.gpsimd.tensor_tensor(heads(xw[:n, :]), heads(xdt[:n, :]), head_scale(n, suf_[:n, c, gh]),
                                            ALU.mult).then_inc(S["xw_ready"], 1)
                    if c > 0:
                        pool.wait_ge(S["state_ready"], g * (NC_ - 1) + c)
                        nc.gpsimd.tensor_tensor(heads(sdec[:, :]), heads(state[:, :]), head_scale(P, tot_[:, c, gh]),
                                                ALU.mult).then_inc(S["state_decay"], 1)
                rhs(g + 1, 0)
            for j in range(1, GX):
                square_sum(pool, GROUPS - 1, j)

        def square_sum(pool, g, j):
            pool.wait_ge(S["gate_sq"], g * GX + j + 1)
            if j > 1:
                pool.wait_ge(S["sq_sum"], g * (GX - 1) + j - 1)
            nc.gpsimd.tensor_tensor(tmp[:, 0, :], tmp[:, 0, :], tmp[:, j, :], ALU.add).then_inc(S["sq_sum"], 1)

        def ssm_dve(dve):
            nc.vector.memset(ones[:, :], 1.0).then_inc(S["set_up"], 1)
            nc.vector.memset(mean_mat[:, :], 1.0 / D).then_inc(S["set_up"], 1)
            nc.vector.memset(pick[:, :, :, :], 0.0).then_inc(S["set_up"], 1)
            dve.wait_ge(S["set_up"], 3)
            for i, n in enumerate(MEAN_OF):
                diagonal = pick[:, i, :, :].rearrange("p c r -> p (c r)")[:, 0:NS * NS:NS + 1]
                nc.vector.memset(diagonal, 1.0 / n).then_inc(S["set_up"], 1)
            for i, e in enumerate((LN_EPS, RMS_EPS)):
                nc.vector.memset(eps[:, i:i + 1], e).then_inc(S["set_up"], 1)
            nc.vector.memset(dtt[:, :, :, :], 0.0).then_inc(S["set_up"], 1)
            nc.vector.memset(ytok[:, :], 0.0).then_inc(S["set_up"], 1)
            for k in range(KT):
                dve.wait_ge(S["h_hi0"], k + 1)
                nc.vector.tensor_tensor(hlo[:, k, :], h[:, k, :], hhi[:, k, :].bitcast(F32), ALU.subtract
                                        ).then_inc(S["h_lo0"], 1)
                if k == 1:
                    prep_lo(dve, 0, 0)
            prep_lo(dve, 1, 1)
            dve.wait_ge(S["const_in"], 16)
            nc.vector.tensor_copy(strict_r[:, :], strict).then_inc(S["set_up"], 1)
            dve.wait_ge(S["set_up"], SET_UP)
            dve.wait_ge(S["dt_mm"], 1)
            dtb = cc("dtb")
            dt_ps = ps[:, 4, 0:NC_ * SSM_HEADS].rearrange("p (c n) -> p c n", c=NC_)
            nc.vector.tensor_tensor(dt_[:META, 0], dt_ps[:META, 0], dtb[:META], ALU.add).then_inc(S["dt_bias"], 1)
            nc.vector.tensor_tensor(dt_[:, 1:], dt_ps[:, 1:], dtb.unsqueeze(1).broadcast_to([P, NC_ - 1, SSM_HEADS]),
                                    ALU.add).then_inc(S["dt_bias"], 1)
            dve.wait_ge(S["dt_act"], 2)
            nc.vector.tensor_scalar(tot_, e_, 1.0, None, ALU.add).then_inc(S["dt_dve"], 1)
            dve.wait_ge(S["dt_dve"], 1)
            nc.vector.scalar_tensor_tensor(acs_, tot_, -1.0, e_, ALU.add, ALU.subtract).then_inc(S["dt_dve"], 1)
            dve.wait_ge(S["dt_act"], 4)
            dve.wait_ge(S["dt_dve"], 2)
            nc.vector.tensor_tensor(suf_, suf_, acs_, ALU.subtract).then_inc(S["dt_dve"], 1)
            dve.wait_ge(S["dt_dve"], 3)
            nc.vector.scalar_tensor_tensor(dt_, dt_, 0.0, suf_, ALU.max, ALU.add).then_inc(S["dt_dve"], 1)
            dve.wait_ge(S["dt_dve"], 4)
            nc.vector.tensor_scalar(negA, negA, -1.0, None, ALU.mult).then_inc(S["dt_dve"], 1)
            dve.wait_ge(S["dt_dve"], 5)
            nc.vector.tensor_tensor(a_, dt_, negA.unsqueeze(1).broadcast_to([P, NC_, SSM_HEADS]),
                                    ALU.mult).then_inc(S["dt_dve"], 1)
            dve.wait_ge(S["dt_dve"], 6)
            nc.vector.tensor_copy(a_parts[:, 0], a_).then_inc(S["dt_dve"], 1)
            dve.wait_ge(S["dt_dve"], 7)
            nc.vector.tensor_tensor(a_parts[:, 1], a_, a_parts[:, 0].bitcast(F32), ALU.subtract
                                    ).then_inc(S["dt_dve"], 1)
            for g in range(GROUPS):
                ssm_group_dve(dve, g)
            norm_dve_gate(dve, GROUPS - 1)
            for half in range(2):
                nc.vector.tensor_tensor(h[:, 4 * half:4 * half + 4, :], hhi[:, 4 * half:4 * half + 4, :].bitcast(F32),
                                        hlo[:, 4 * half:4 * half + 4, :].bitcast(F32), ALU.add
                                        ).then_inc(S["out_evac"], 1)

        def taps(dve, dst, bank_pair, weight, ntaps, tap_count, t0=0):
            for i in range(1, ntaps):
                if i > 1:
                    dve.wait_ge(S["conv_tap"], tap_count + i - 1)
                op = nc.vector.scalar_tensor_tensor(dst[:, t0 + i:T], pair(bank_pair, t0=t0)[:, 0:T - t0 - i],
                                                    weight(i), dst[:, t0 + i:T],
                                                    ALU.mult, ALU.add)
                op.then_inc(S["conv_taps"] if i == ntaps - 1 else S["conv_tap"], 1)

        def head_scale(n, per_head):
            return per_head.unsqueeze(2).broadcast_to([n, GH, HD])

        def heads(ap):
            return ap.rearrange("p (a d) -> p a d", a=GH)

        def ssm_group_dve(dve, g):
            q = g % 2
            dst = [bT[:, :], cT[:, :]] + [xy[:, q, j, :] for j in range(GX)]
            if g > 0:
                norm_dve_gate(dve, g - 1)
            for j in range(NX):
                n = g * GT + j
                dve.wait_ge(S["conv_first"], g * NX + j + 1)
                taps(dve, dst[j], j % 2, lambda i: cw[:, n:n + 1, TAPS - 1 - i], TAPS, (g * NX + j) * (TAPS - 2))
                prep_lo(dve, n + 2, (n + 2) % RAW)
                if g > 0 and j == 3:
                    stat_rec(dve, g - 1)
                if g > 0 and j == 4:
                    norm_dve_scale(dve, g - 1)
                if g > 0 and j == 5:
                    norm_dve_lo(dve, g - 1)

            for kind, c in IN_DVE:
                u = g * NC_ + c
                if kind == "z":
                    n = g * GT + NX + c
                    prep_lo(dve, n + 2, (n + 2) % RAW)
                    continue
                t0, n = CH[c]
                gh = slice(g * GH, (g + 1) * GH)
                done = S["ssd_local"]
                if kind == "in":
                    dve.wait_ge(S["ssd_in"], u + 1)
                    nc.vector.tensor_tensor(heads(xdt[:n, :]), heads(ps[:n, 4, :]), head_scale(n, dt_[:n, c, gh]),
                                            ALU.mult).then_inc(done, 1)
                    dve.wait_ge(S["btok_ready"], u + 1)
                    nc.vector.tensor_tensor(cbm[:n, :n], ps[:n, 5, P:P + n], triu[:n, :n], ALU.mult).then_inc(done, 1)
                    dve.wait_ge(S["decay_exp"], u + 1)
                    dve.wait_ge(done, u * 3 + 2)
                    nc.vector.tensor_tensor(decay[c], decay[c], cbm[:n, :n].unsqueeze(1).broadcast_to([n, GH, n]),
                                            ALU.mult).then_inc(done, 1)
                elif kind == "out":
                    if c < NC_ - 1:
                        dve.wait_ge(S["ssd_state"], g * (NC_ - 1) + c + 1)
                    if c == 0:
                        nc.vector.tensor_copy(state[:, :], ps[:, 2, :]).then_inc(S["state_ready"], 1)
                        dve.wait_ge(S["ssd_out"], u + 1)
                        nc.vector.tensor_copy(ytok[:n, :], ps[:n, 6, :]).then_inc(S["ytok_ready"], 1)
                        continue
                    if c < NC_ - 1:
                        dve.wait_ge(S["state_decay"], g * (NC_ - 2) + c)
                        dve.wait_ge(S["ssd_yoff"], g * (NC_ - 1) + c)
                        nc.vector.tensor_tensor(state[:, :], sdec[:, :], ps[:, 2, :], ALU.add
                                                ).then_inc(S["state_ready"], 1)
                    dve.wait_ge(S["ssd_yoff"], g * (NC_ - 1) + c)
                    nc.vector.tensor_tensor(heads(ytok[:n, :]), heads(ps[:n, 7, :]),
                                            head_scale(n, acs_[:n, c, gh]), ALU.mult).then_inc(S["yoff"], 1)
                    dve.wait_ge(S["yoff"], g * (NC_ - 1) + c)
                    dve.wait_ge(S["ssd_out"], u + 1)
                    nc.vector.tensor_tensor(ytok[:n, :], ytok[:n, :], ps[:n, 6, :], ALU.add
                                            ).then_inc(S["ytok_ready"], 1)
                else:
                    dve.wait_ge(S["ssd_back"], u + 1)
                    for j in range(GX):
                        nc.vector.scalar_tensor_tensor(xy[:, q, j, t0:t0 + n], xy[:, q, j, t0:t0 + n],
                                                       dsk[:, g * GX + j:g * GX + j + 1], ps[:, 3, j * P:j * P + n],
                                                       ALU.mult, ALU.add).then_inc(S["y_ready"], 1)

        def norm_dve_gate(dve, g):
            dve.wait_ge(S["y_ready"], g * (NC_ * GX) + NC_ * GX)
            for j in range(GX):
                dve.wait_ge(S["z_silu"], g * GX + j + 1)
                nc.vector.tensor_tensor(xy[:, g % 2, j, :], xy[:, g % 2, j, :], tmp[:, j, :], ALU.mult
                                        ).then_inc(S["gate_mul"], 1)

        def norm_dve_scale(dve, g):
            dve.wait_ge(S["st_bc"], g + 1)
            for j in range(GX):
                dve.wait_ge(S["gate_sq"], g * GX + j + 1)
                nc.vector.tensor_tensor(xy[:, g % 2, j, :], xy[:, g % 2, j, :], pair(3), ALU.mult
                                        ).then_inc(S["rms_scale"], 1)

        def norm_dve_lo(dve, g):
            for j in range(GX):
                t = g * GX + j
                dve.wait_ge(S["rms_hi"], t + 1)
                nc.vector.scalar_tensor_tensor(ynlo[:, t, :], xy[:, g % 2, j, :], ng[:, t:t + 1],
                                               ynhi[:, t, :].bitcast(F32), ALU.mult, ALU.subtract
                                               ).then_inc(S["rms_lo"], 1)

        def out_steps(base, per, body, run, straight=False, loop=None):
            def step(it):
                for m in range(body):
                    for s in range(per):
                        idx = m * per + s
                        run(base + it * (body * per) + idx, (base + idx) % RAW, it * body + m, m, s)
            if straight:
                for it in range(KT // body):
                    step(it)
            else:
                with loop(0, KT // body) as it:
                    step(it)

        def out_pe(pe, base, per, number, sizes, xhi, xlo, body, straight, before_k, t0=0):
            def run(n, pos, m, mq, s):
                pe.wait_ge(S["w_lo"], n + 1)
                if s == 0:
                    pe.wait_ge(S["out_evac"], m + (KT * number + 1))
                product(pos % 2, sizes[s], xhi, xlo, KT * s, mq % 2, s == 0, s == per - 1,
                        before_k=lambda k: before_k(KT * s + k), t0=t0).then_inc(S["w_used"], 1)
            out_steps(base, per, body, run, straight, pe.Fori)

        def mix_out_pe(pe):
            def share(idx, part=(0, 1)):
                m, s = MIX_ORDER[idx]
                return product((W_MOUT + idx) % 2, KT, ynhi, ynlo, KT * s, m % 2, s == 0, s == 1, part=part)

            pe.wait_ge(S["w_lo"], W_MOUT + 1)
            pe.wait_ge(S["z_silu"], GROUPS * GX)
            pe.wait_ge(S["rms_lo"], (GROUPS - 1) * GX)
            share(0).then_inc(S["w_used"], 1)
            pe.wait_ge(S["w_lo"], W_MOUT + 2)
            pe.wait_ge(S["y_ready"], GROUPS * NC_ * GX)
            share(1, (0, 2))
            norm_pe_sum(pe, GROUPS - 1)
            share(1, (1, 2)).then_inc(S["w_used"], 1)
            stat_spread(pe, GROUPS - 1, 3)
            for idx in (2, 3):
                pe.wait_ge(S["w_lo"], W_MOUT + idx + 1)
                share(idx, (0, 2))
            pe.wait_ge(S["rms_lo"], GROUPS * GX)
            for idx in (2, 3):
                share(idx, (1, 2)).then_inc(S["w_used"], 1)
            for idx in range(4, N_MOUT):
                m, s = MIX_ORDER[idx]
                pe.wait_ge(S["w_lo"], W_MOUT + idx + 1)
                if s == 0:
                    pe.wait_ge(S["out_evac"], m + 1)
                share(idx).then_inc(S["w_used"], 1)

        def mix_out_act(act):
            norm_act_sq(act, GROUPS - 1, 1)
            for n in range(W_MOUT, W_MOUT + N_MOUT):
                prep_hi(act, n + 2, (n + 2) % RAW)
                if n == W_MOUT:
                    stat_sqrt(act, GROUPS - 1, 3, 1)
                if n == W_MOUT + 1:
                    norm_act_hi(act, GROUPS - 1, 1)

        def mix_out_dve(dve):
            for idx, (m, s) in enumerate(MIX_ORDER):
                n = W_MOUT + idx
                if idx == 1:
                    stat_rec(dve, GROUPS - 1)
                    norm_dve_scale(dve, GROUPS - 1)
                if s == 1:
                    dve.wait_ge(S["w_used"], n + 1)
                    nc.vector.scalar_tensor_tensor(h[:, m, :], h[:, m, :], ALPHA, pair(m % 2), ALU.mult, ALU.add
                                                   ).then_inc(S["out_evac"], 1)
                prep_lo(dve, n + 2, (n + 2) % RAW)
                if idx == 1:
                    norm_dve_lo(dve, GROUPS - 1)

        def out_act(act, base, per, body, straight):
            def run(n, pos, m, mq, s):
                if not isinstance(n, int) or n + 2 < end:
                    prep_hi(act, n + 2, (pos + 2) % RAW)
            out_steps(base, per, body, run, straight, act.Fori)

        def out_dve(dve, base, per, body, straight, t0=0):
            def run(n, pos, m, mq, s):
                if s == per - 1:
                    dve.wait_ge(S["w_used"], n + 1)
                    hm = h[:, bass.ds(m, 1), t0:T] if not isinstance(m, int) else h[:, m:m + 1, t0:T]
                    nc.vector.scalar_tensor_tensor(hm, hm, ALPHA, pair(mq % 2, t0=t0).unsqueeze(1), ALU.mult, ALU.add
                                                   ).then_inc(S["out_evac"], 1)
                if not isinstance(n, int) or n + 2 < end:
                    prep_lo(dve, n + 2, (pos + 2) % RAW)
            out_steps(base, per, body, run, straight, dve.Fori)

        FFN_T0 = (0, (META - (FTAPS - 1)) // 4 * 4)

        def two_products(pe, n, L, t0=0):
            pe.wait_ge(S["w_lo"], n + 2)
            for k in range(KT + 2):
                if k < KT:
                    stream_ready(pe, L, k)
                for i, kk in enumerate((k, k - 2)):
                    if 0 <= kk < KT:
                        mm = product((n + i) % 2, KT, hhi, hlo, 0, i, part=(kk, KT), t0=t0)
                        if kk == KT - 1:
                            mm.then_inc(S["w_used"], 1)

        def ffn_pe(pe, L, base):
            def tile(n, q, taps_wait):
                pe.wait_ge(S["w_lo"], n + 1)
                pe.wait_ge(S["conv_taps"], taps_wait)
                product((base + q) % 2, KT, hhi, hlo, 0, q % 2, t0=FFN_T0[L]).then_inc(S["w_used"], 1)

            two_products(pe, base, LN_OF_FFN[L], FFN_T0[L])
            for q in range(2, 4):
                tile(base + q, q, TAP0 + L * N_FIN + q - 1)
            with pe.Fori(1, N_FIN // 4) as it:
                for q in range(4):
                    tile(base + it * 4 + q, q, it * 4 + (TAP0 + L * N_FIN + q - 1))

        def ffn_act(act, L, base):
            t0 = FFN_T0[L]
            with act.Fori(0, N_FIN // 4) as it:
                for q in range(4):
                    n = base + it * 4 + q
                    v = it * 4 + (L * N_FIN + q)
                    prep_hi(act, n + 2, (base + q + 2) % RAW)
                    act.wait_ge(S["w_used"], n + 1)
                    nc.scalar.activation(tmp[:, q, t0:], pair(q % 2, t0=t0), ACT.Identity, bias=fb[:, bass.ds(v, 1)],
                                         scale=fw[:, bass.ds(v, 1), FTAPS - 1]).then_inc(S["conv_first"], 1)
                    if q % 2:
                        j = it * 2 + (L * FT + q // 2)
                        act.wait_ge(S["conv_taps"], v + TAP0)
                        nc.scalar.activation(tmp[:, q - 1, t0:], tmp[:, q - 1, t0:], ACT.Silu).then_inc(S["ffn_silu"], 1)
                        act.wait_ge(S["ffn_mul"], j + 1)
                        nc.scalar.activation(ahi[:, bass.ds(it * 2 + q // 2, 1), t0:], tmp[:, q - 1:q, t0:], ACT.Copy
                                             ).then_inc(S["ffn_hi"], 1)

        def ffn_dve(dve, L, base):
            t0 = FFN_T0[L]
            with dve.Fori(0, N_FIN // 4) as it:
                for q in range(4):
                    n = base + it * 4 + q
                    v = it * 4 + (L * N_FIN + q)
                    prep_lo(dve, n + 2, (base + q + 2) % RAW)
                    dve.wait_ge(S["conv_first"], v + TAP0 + 1)
                    taps(dve, tmp[:, q, :], q % 2, lambda i: fw[:, bass.ds(v, 1), FTAPS - 1 - i], FTAPS,
                         v * (FTAPS - 2) + TAP0 * (TAPS - 2), t0)
                    if q % 2:
                        j = it * 2 + (L * FT + q // 2)
                        dve.wait_ge(S["ffn_silu"], j + 1)
                        dve.wait_ge(S["conv_taps"], v + TAP0 + 1)
                        nc.vector.tensor_tensor(tmp[:, q - 1, t0:], tmp[:, q - 1, t0:], tmp[:, q, t0:], ALU.mult
                                                ).then_inc(S["ffn_mul"], 1)
                        dve.wait_ge(S["ffn_hi"], j + 1)
                        jl = bass.ds(it * 2 + q // 2, 1)
                        nc.vector.tensor_tensor(alo[:, jl, t0:], tmp[:, q - 1:q, t0:], ahi[:, jl, t0:].bitcast(F32),
                                                ALU.subtract).then_inc(S["ffn_lo"], 1)

        TAP0 = GROUPS * (2 + GX)
        LN_OF_FFN = (0, 2)
        fout = (KT, KT, FT - 2 * KT)

        N_CKV, N_CQ = KVL // P, QL // P
        N_C = N_CKV + N_CQ
        SQ = [tmp[:, i, :] for i in range(4)] + [qst[:, 0, 0, :]]
        DOWN_LN = 1
        V_STEPS = 2 * KEY_TILES

        RMS_SUM, RMS_SCALE = (2, 5), (3, 6)
        RMS_TILES = ((0, N_CKV), (N_CKV, N_C))

        def down_pe(pe):
            two_products(pe, W_DOWN, DOWN_LN)
            for t in range(2, N_DOWN):
                n = W_DOWN + t
                pe.wait_ge(S["w_lo"], n + 1)
                pe.wait_ge(S["down_copy"], t - 1)
                product(n % 2, KT, hhi, hlo, 0, t % 2).then_inc(S["w_used"], 1)
                if t in RMS_SUM:
                    i = RMS_SUM.index(t)
                    t0, t1 = RMS_TILES[i]
                    stats_mm(pe, SQ[t0:t1], 2 + i, 2 + i, lambda k: pe.wait_ge(S["down_sq"], t0 + k + 1)
                             ).then_inc(S["st_mm"], 1)
                if t in RMS_SCALE:
                    i = RMS_SCALE.index(t)
                    stat_spread(pe, ST_RMS[i], 2 + i)
            pe.wait_ge(S["w_lo"], W_V + N_V)
            pe.wait_ge(S["rms_lo"], GROUPS * GX + N_CKV)
            pe.wait_ge(S["kpe"], 2)
            pe.wait_ge(S["down_copy"], N_C)
            def v_share(v, kt):
                t0, half = P * (v // 2), v % 2
                n = min(P, T - t0)
                slot = (W_V + kt) % 2
                for p, (x, w) in enumerate(((chi, whi), (clo, whi), (chi, wlo))):
                    mm = nc.tensor.matmul(ps[:n, v % 4, :], x[:, kt, t0:t0 + n],
                                          w[:, slot, half * BANK:(half + 1) * BANK],
                                          start=kt == 0 and p == 0, stop=kt == N_V - 1 and p == 2)
                return mm

            for v in range(V_STEPS - 4):
                if v >= 4:
                    pe.wait_ge(S["v_evac"], v - 3)
                for kt in range(N_V):
                    mm = v_share(v, kt)
                mm.then_inc(S["v_mm"], 1)
            pe.wait_ge(S["v_evac"], V_STEPS - 4)
            for kt in range(N_V):
                for v in range(V_STEPS - 4, V_STEPS):
                    mm = v_share(v, kt)
                    if kt == N_V - 1 and v < V_STEPS - 1:
                        mm.then_inc(S["v_mm"], 1)
                mm.then_inc(S["w_used"], 1)

        def latent_gain(c):
            return cc("kvg")[:, c:c + 1] if c < N_CKV else cc("qg")[:, c - N_CKV:c - N_CKV + 1]

        def down_act(act):
            for t in range(N_DOWN):
                n = W_DOWN + t
                prep_hi(act, n + 2, (n + 2) % RAW)
                if t < N_C:
                    act.wait_ge(S["w_used"], n + 1)
                    nc.scalar.activation(craw[:, t, :], pair(t % 2), ACT.Copy).then_inc(S["down_copy"], 1)
                    act.wait_ge(S["down_copy"], t + 1)
                    nc.scalar.activation(SQ[t], craw[:, t, :], ACT.Square).then_inc(S["down_sq"], 1)
                if t in RMS_SUM:
                    stat_sqrt(act, ST_RMS[RMS_SUM.index(t)], 2 + RMS_SUM.index(t), 1)
                if t in RMS_SCALE:
                    for c in range(*RMS_TILES[RMS_SCALE.index(t)]):
                        act.wait_ge(S["rms_scale"], GROUPS * GX + c + 1)
                        nc.scalar.activation(chi[:, c, :], craw[:, c, :], ACT.Copy, scale=latent_gain(c)
                                             ).then_inc(S["rms_hi"], 1)
            act.wait_ge(S["att_zero"], ZEROED)
            for v in range(V_STEPS):
                n = min(P, T - P * (v // 2))
                act.wait_ge(*((S["v_mm"], v + 1) if v < V_STEPS - 1 else (S["w_used"], W_PAIR)))
                nc.scalar.activation(vtok[:n, v // 2, (v % 2) * BANK:(v % 2 + 1) * BANK], ps[:n, v % 4, :], ACT.Copy
                                     ).then_inc(S["v_evac"], 1)
            for i in range(N_V):
                prep_hi(act, W_PAIR + i, (W_PAIR + i) % RAW)

        ZEROED = NC_ + 1

        def down_dve(dve):
            for i in range(NC_):
                nc.vector.memset(prob[i][:, :, keys(i):], 0.0).then_inc(S["att_zero"], 1)
            nc.vector.memset(vtok[:, KEY_TILES - 1, :], 0.0).then_inc(S["att_zero"], 1)
            for t in range(N_DOWN):
                n = W_DOWN + t
                prep_lo(dve, n + 2, (n + 2) % RAW)
                if t >= N_C:
                    if t == N_C:
                        dve.wait_ge(S["tab_in"], 16)
                    dve.wait_ge(S["w_used"], n + 1)
                    nc.vector.tensor_tensor(kst[NOPE:, 0, t - N_C, :], pair(t % 2)[NOPE:], tab[NOPE:, 1 + t - N_C, :],
                                            ALU.mult).then_inc(S["kpe"], 1)
                if t in RMS_SUM:
                    stat_rec(dve, ST_RMS[RMS_SUM.index(t)])
                if t in RMS_SCALE:
                    i = RMS_SCALE.index(t)
                    dve.wait_ge(S["st_bc"], ST_RMS[i] + 1)
                    for c in range(*RMS_TILES[i]):
                        nc.vector.tensor_tensor(craw[:, c, :], craw[:, c, :], pair(2 + i), ALU.mult
                                                ).then_inc(S["rms_scale"], 1)
                    for c in range(*RMS_TILES[i]):
                        dve.wait_ge(S["rms_hi"], GROUPS * GX + c + 1)
                        nc.vector.scalar_tensor_tensor(clo[:, c, :], craw[:, c, :], latent_gain(c),
                                                       chi[:, c, :].bitcast(F32), ALU.mult, ALU.subtract
                                                       ).then_inc(S["rms_lo"], 1)
            dve.wait_ge(S["kpe"], 2)
            nc.vector.tensor_tensor(kst[NOPE:, 0, 0, :], kst[NOPE:, 0, 0, :], kst[NOPE:, 0, 1, :], ALU.add
                                    ).then_inc(S["kpe"], 1)
            dve.wait_ge(S["kpe"], 3)
            for b, a in ((0, 1), (1, 0), (1, 1)):
                nc.vector.tensor_copy(kst[NOPE:, b, a, :], kst[NOPE:, 0, 0, :]).then_inc(S["kpe"], 1)
            for i in range(N_V):
                prep_lo(dve, W_PAIR + i, (W_PAIR + i) % RAW)

        UNITS = ((4, 0), (0, 0), (4, 1), (0, 1), (3, 0), (1, 0), (3, 1), (1, 1), (2, 0), (2, 1))
        NU = len(UNITS)
        LAST = N_PAIR * NU
        S_EVEN, S_ODD, PV_BANK, PT_BANK, PROJ = 0, 2, 3, 4, 3
        assert all(i < NC_ - 1 for i, _ in UNITS[1::2])

        def keys(i):
            t0, n = CH[i]
            return t0 + n

        def scores(x):
            n = keys(UNITS[x % NU][0])
            at = (S_ODD if x % 2 else S_EVEN) * BANK
            return psf[:, at:at + n] if n <= BANK else psf[:, at + LEFT:at + LEFT + n]

        def pt_taken(eng, x):
            eng.wait_ge(*((S["pt_dve"], x // 2 + 1) if x % 2 else (S["pt_act"], x // 2 + 1)))

        OT_AT = 2 * PROJ * BANK + BANK - CH[-1][0]
        PROJ_STEPS = {2: ((0, 0, 1),), 3: ((1, 0, 3), (1, 1, 3)), 4: ((1, 2, 3),), 5: ((2, 0, 3), (2, 1, 3)),
                      6: ((2, 2, 3),)}

        def proj_at(pr, which):
            return 2 if (pr, which) == (0, 1) else PROJ

        def project(pe, pr, which, share, shares):
            n = W_PAIR + pr
            if share == 0:
                if which == 0:
                    pe.wait_ge(S["w_lo"], n + 1)
                if which == (1 if pr else 2):
                    pe.wait_ge(S["k_evac"], pr * 2 + 2)
                if which == 2 and pr:
                    pe.wait_ge(S["q_evac"], pr * 2 + 1)
            col = (0, N_CKV, N_CKV + N_CQ)[which] * P
            mm = product(n % 2, N_CQ if which else N_CKV, chi, clo, N_CKV if which else 0, proj_at(pr, which), col=col,
                         part=(share, shares))
            if share == shares - 1:
                mm.then_inc(S["w_used"] if which == 2 else S["proj_mm"], 1)

        def score(pe, x):
            if x >= LAST:
                return
            pr, u = divmod(x, NU)
            i, a = UNITS[u]
            if u == 0:
                pe.wait_ge(S["k_evac"], pr * 2 + 2)
                pe.wait_ge(S["q_evac"], pr * 2 + 1)
            if u == 2:
                pe.wait_ge(S["q_evac"], pr * 2 + 2)
            t0, nk = CH[i][0], keys(i)
            out = scores(x)
            for k0, k1 in [(0, nk)] if nk <= BANK else [(0, HALF), (HALF, nk)]:
                mm = nc.tensor.matmul(out[:, k0:k1], qst[:, pr % 2, a, t0:t0 + P], kst[:, pr % 2, a, k0:k1],
                                      start=True, stop=i == 0, skip_group_check=True)
            if i:
                mm = nc.tensor.matmul(out[:64, nk - 64:nk], cc("one")[0:1, :], cc("neg")[0:1, :],
                                      start=False, stop=True, skip_group_check=True)
            mm.then_inc(S["s_mm"], 1)

        def unit_out(pe, x):
            pr, u = divmod(x, NU)
            i, a = UNITS[u]
            pt_taken(pe, x)
            if x > 0:
                pe.wait_ge(S["pv_evac"], x)
            for j in range(i + 1):
                mm = nc.tensor.matmul(ps[:, PV_BANK, 0:VH], probT[:, x % 2, j, :],
                                      vtok[:, j, (pr * 2 + a) * VH:(pr * 2 + a + 1) * VH],
                                      start=j == 0, stop=j == i)
            mm.then_inc(S["pv_mm"], 1)

        def o_back(pe, pr):
            pe.wait_ge(S["pv_evac"], (pr + 1) * NU)
            for i, (t0, n2) in enumerate(CH):
                mm = nc.tensor.transpose(psf[:, OT_AT + t0:OT_AT + t0 + n2], otok[:n2, pr % 2, i, :],
                                         ident[:n2, :n2])
            mm.then_inc(S["ot_mm"], 1)

        def att_pe(pe):
            for which in range(3):
                project(pe, 0, which, 0, 1)
            pe.wait_ge(S["v_evac"], V_STEPS)
            score(pe, 0)
            score(pe, 1)
            for x in range(LAST):
                pr, u = divmod(x, NU)
                pe.wait_ge(S["s_exp"], x + 1)
                if x > 0:
                    pt_taken(pe, x - 1)
                for j in range(UNITS[u][0] + 1):
                    mm = nc.tensor.transpose(ps[:, PT_BANK + j // 4, (j % 4) * P:(j % 4 + 1) * P],
                                             prob[UNITS[u][0]][:, UNITS[u][1], j * P:(j + 1) * P], ident)
                mm.then_inc(S["pt_mm"], 1)
                score(pe, x + 2)
                if x > 0:
                    unit_out(pe, x - 1)
                if u == 1 and pr > 0:
                    pe.wait_ge(S["q_evac"], pr * 2 + 2)
                    o_back(pe, pr - 1)
                if pr < N_PAIR - 1:
                    if u == 2 and pr > 0:
                        pe.wait_ge(S["ot_lo"], pr)
                    for share in PROJ_STEPS.get(u, ()):
                        project(pe, pr + 1, *share)
            unit_out(pe, LAST - 1)
            o_back(pe, N_PAIR - 1)

        def evac_k(act, pr):
            act.wait_ge(S["proj_mm"], pr * 2 + 1)
            for a in range(2):
                nc.scalar.activation(kst[:NOPE, pr % 2, a, :], pair(PROJ)[a * NOPE:(a + 1) * NOPE], ACT.Copy
                                     ).then_inc(S["k_evac"], 1)

        def evac_q(dve, pr, a):
            dve.wait_ge(*((S["proj_mm"], pr * 2 + 2) if a == 0 else (S["w_used"], W_PAIR + pr + 1)))
            nc.vector.tensor_tensor(qst[:, pr % 2, a, :], pair(proj_at(pr, 1 + a)), tab[:, 0, :], ALU.mult).then_inc(S["q_evac"], 1)

        def evac_o_hi(act, pr):
            act.wait_ge(S["ot_mm"], pr + 1)
            nc.scalar.activation(hhi[:, pr, :], psf[:, OT_AT:OT_AT + T], ACT.Copy).then_inc(S["ot_hi"], 1)

        def evac_o_lo(dve, pr):
            dve.wait_ge(S["ot_hi"], pr + 1)
            nc.vector.tensor_tensor(hlo[:, pr, :], psf[:, OT_AT:OT_AT + T], hhi[:, pr, :].bitcast(F32),
                                    ALU.subtract).then_inc(S["ot_lo"], 1)

        def copy_pt(copy, x):
            n = UNITS[x % NU][0] + 1
            return copy(probT[:, x % 2, 0:n, :],
                        psf[:, PT_BANK * BANK:PT_BANK * BANK + n * P].rearrange("p (j q) -> p j q", j=n))

        def exponentials(act, x):
            if x >= LAST:
                return
            i, a = UNITS[x % NU]
            act.wait_ge(S["s_max"], x + 1)
            nc.scalar.activation(prob[i][:, a, :keys(i)], scores(x), ACT.Exp, bias=nmax[:, x % 4, 0:1],
                                 accum_out=nmax[:, x % 4, 1:2]).then_inc(S["s_exp"], 1)

        def att_act(act):
            evac_k(act, 0)
            exponentials(act, 0)
            for x in range(LAST):
                pr, u = divmod(x, NU)
                exponentials(act, x + 1)
                if x % 2 == 0:
                    act.wait_ge(S["pt_mm"], x + 1)
                    copy_pt(lambda to, frm: nc.scalar.activation(to, frm, ACT.Copy), x).then_inc(S["pt_act"], 1)
                if u == 1 and pr > 0:
                    evac_o_hi(act, pr - 1)
                if u == 2 and pr < N_PAIR - 1:
                    evac_k(act, pr + 1)
                if u == 7:
                    prep_hi(act, W_PAIR + pr + 2, (W_PAIR + pr + 2) % RAW)
            evac_o_hi(act, N_PAIR - 1)

        def att_dve(dve):
            for a in range(2):
                evac_q(dve, 0, a)

            def row_max(x):
                if x < LAST:
                    dve.wait_ge(S["s_mm"], x + 1)
                    nc.vector.tensor_reduce(nmax[:, x % 4, 0:1], scores(x), axis=AX.X, op=ALU.max, negate=True
                                            ).then_inc(S["s_max"], 1)

            def evac_out(x):
                pr, u = divmod(x, NU)
                i, a = UNITS[u]
                dve.wait_ge(S["pv_mm"], x + 1)
                dve.wait_ge(S["s_rec"], x + 1)
                nc.vector.tensor_scalar(otok[:, pr % 2, i, a * VH:(a + 1) * VH], ps[:, PV_BANK, 0:VH],
                                        nmax[:, x % 4, 2:3], None, ALU.mult).then_inc(S["pv_evac"], 1)
            row_max(0)
            row_max(1)
            for x in range(LAST):
                pr, u = divmod(x, NU)
                dve.wait_ge(S["s_exp"], x + 1)
                nc.vector.reciprocal(nmax[:, x % 4, 2:3], nmax[:, x % 4, 1:2]).then_inc(S["s_rec"], 1)
                if x % 2:
                    dve.wait_ge(S["pt_mm"], x + 1)
                    copy_pt(nc.vector.tensor_copy, x).then_inc(S["pt_dve"], 1)
                row_max(x + 2)
                if x > 0:
                    evac_out(x - 1)
                if u == 1 and pr > 0:
                    evac_o_lo(dve, pr - 1)
                if u in (4, 6) and pr < N_PAIR - 1:
                    evac_q(dve, pr + 1, 0 if u == 4 else 1)
                if u == 7:
                    prep_lo(dve, W_PAIR + pr + 2, (W_PAIR + pr + 2) % RAW)
            evac_out(LAST - 1)
            evac_o_lo(dve, N_PAIR - 1)

        def hidden_ready(pe, L):
            def wait(k):
                if k % KT == 0:
                    pe.wait_ge(S["ffn_lo"], L * FT + min(k + KT, FT))
            pe.wait_ge(S["conv_taps"], TAP0 + (L + 1) * N_FIN - 1)
            return wait

        def o_ready(pe):
            return lambda k: pe.wait_ge(S["ot_lo"], k + 1)

        @block.tensor
        def _(pe):
            ssm_pe(pe)
            mix_out_pe(pe)
            ln_pe(pe, 0)
            if STOP >= 2:
                ffn_pe(pe, 0, W_FIN0)
                out_pe(pe, W_FOUT0, 3, 1, fout, ahi, alo, OUT_BODY, False, hidden_ready(pe, 0))
                ln_pe(pe, 1)
            if STOP >= 3:
                down_pe(pe)
                att_pe(pe)
                out_pe(pe, W_O, 1, 2, (KT,), hhi, hlo, OUT_BODY, False, o_ready(pe))
                ln_pe(pe, 2)
            if STOP > 3:
                ffn_pe(pe, 1, W_FIN1)
                out_pe(pe, W_FOUT1, 3, 3, fout, ahi, alo, OUT_BODY, True, hidden_ready(pe, 1), META)
                ln_pe(pe, 3)

        @block.scalar
        def _(act):
            ssm_act(act)
            mix_out_act(act)
            ln_act(act, 0)
            if STOP >= 2:
                ffn_act(act, 0, W_FIN0)
                out_act(act, W_FOUT0, 3, OUT_BODY, False)
                ln_act(act, 1)
            if STOP >= 3:
                down_act(act)
                att_act(act)
                out_act(act, W_O, 1, OUT_BODY, False)
                ln_act(act, 2)
            if STOP > 3:
                ffn_act(act, 1, W_FIN1)
                out_act(act, W_FOUT1, 3, OUT_BODY, True)
                ln_act(act, 3)

        @block.vector
        def _(dve):
            ssm_dve(dve)
            mix_out_dve(dve)
            ln_dve(dve, 0)
            if STOP >= 2:
                ffn_dve(dve, 0, W_FIN0)
                out_dve(dve, W_FOUT0, 3, OUT_BODY, False)
                ln_dve(dve, 1)
            if STOP >= 3:
                down_dve(dve)
                att_dve(dve)
                out_dve(dve, W_O, 1, OUT_BODY, False)
                ln_dve(dve, 2)
            if STOP > 3:
                ffn_dve(dve, 1, W_FIN1)
                out_dve(dve, W_FOUT1, 3, OUT_BODY, True, META)
                ln_dve(dve, 3)

        @block.gpsimd
        def _(pool):
            ssm_pool(pool)
            h_sum_pool(pool, 0)
            ln_pool(pool, 0)
            if STOP >= 2:
                h_sum_pool(pool, 1)
            if STOP >= 3:
                pool.wait_ge(S["w_used"], W_DOWN)
                pool.dma_start(tab[:, :, :], tabs).then_inc(S["tab_in"], 16)
            if STOP >= 2:
                ln_pool(pool, 1)
            if STOP >= 3:
                h_sum_pool(pool, 2)
                ln_pool(pool, 2)
            if STOP > 3:
                h_sum_pool(pool, 3)


def weight_tiles(w):
    k, n = w.shape
    return w.reshape(k // P, P, n // P, P).transpose(2, 1, 0, 3).reshape(n // P, P, k)


def columns(v):
    return np.moveaxis(v.reshape(v.shape[:-1] + (-1, P)), -1, 0)


def weight_stream(m_w_in, m_w_out, kv_w_down, kv_w_up, q_w_down, q_w_up, o_w, f_w_in, f_w_out):
    ssm = weight_tiles(m_w_in[0][:, :2 * INNER + 2 * GROUPS * STATE])
    z, x = ssm[:GROUPS * GX], ssm[GROUPS * GX:2 * GROUPS * GX]
    b, c = (ssm[2 * GROUPS * GX + i * GROUPS:2 * GROUPS * GX + (i + 1) * GROUPS] for i in range(2))
    parts = []
    for g in range(GROUPS):
        parts += [b[g:g + 1], c[g:g + 1], x[g * GX:(g + 1) * GX], z[g * GX:(g + 1) * GX]]
    parts.append(weight_tiles(m_w_out[0]).reshape(N_MOUT, P, WT))

    def ffn(layer):
        w = weight_tiles(f_w_in[layer])
        parts.append(np.stack([w[:FT], w[FT:]], 1).reshape(N_FIN, P, WT))
        o = np.zeros((KT, P, 3 * WT), w.dtype)
        o[:, :, :F] = weight_tiles(f_w_out[layer])
        parts.append(o.reshape(KT, P, 3, WT).transpose(0, 2, 1, 3).reshape(N_FOUT, P, WT))

    mix = weight_tiles(m_w_out[0]).reshape(KT, P, 2, WT)
    parts[-1] = np.stack([mix[m, :, s] for m, s in MIX_ORDER])
    ffn(0)
    pe = kv_w_down[:, KVL:]
    sw = np.concatenate([pe[:, ROPE // 2:], pe[:, :ROPE // 2]], 1)
    down = np.concatenate([kv_w_down[:, :KVL], q_w_down[0]] + [pe] * 4 + [sw] * 4, 1)
    parts.append(weight_tiles(down))
    up = kv_w_up.reshape(KVL // P, P, HEADS, NOPE + VH)
    parts.append(up[..., NOPE:].reshape(KVL // P, P, HEADS * VH))
    kn = up[..., :NOPE].reshape(KVL // P, P, HEADS // 2, 2 * NOPE)
    q = q_w_up[0].reshape(QL // P, P, HEADS, NOPE + ROPE)
    q = np.concatenate([q, q[..., NOPE + ROPE // 2:], q[..., NOPE:NOPE + ROPE // 2]], -1)
    q = q.transpose(2, 1, 0, 3).reshape(HEADS // 2, 2, P, QL // P * P)
    pairs = np.concatenate([kn.transpose(2, 1, 0, 3).reshape(HEADS // 2, P, KVL // P * P), q[:, 0], q[:, 1]], -1)
    parts.append(pairs)
    parts.append(weight_tiles(o_w[0]))
    ffn(1)
    return np.ascontiguousarray(np.concatenate(parts, 0))


def constants(m_w_in, m_conv_w, m_conv_b, m_dt_bias, m_a_log, m_d, m_norm_g, kv_norm_g, q_norm_g,
              f_conv_w, f_conv_b, ln_g, ln_b):
    f = np.float32
    out = np.zeros((P, NCON), f)

    def put(name, v):
        out[:, CC[name][0]:CC[name][1]] = v.reshape(P, -1)
    r = np.arange(P)
    put("ident", np.eye(P, dtype=f))
    put("triu", (r[:, None] <= r[None, :]).astype(f))
    put("strict", (r[:, None] > r[None, :]).astype(f))
    put("wdt", m_w_in[0][:, 2 * INNER + 2 * GROUPS * STATE:].reshape(KT, P, SSM_HEADS).transpose(1, 0, 2))
    put("dtb", np.broadcast_to(m_dt_bias[0], (P, SSM_HEADS)))
    put("alog", np.broadcast_to(m_a_log[0], (P, SSM_HEADS)))
    cw, cb = columns(m_conv_w[0]), columns(m_conv_b[0])
    w, b = np.zeros((P, N_SSM, TAPS), f), np.zeros((P, N_SSM), f)
    for g in range(GROUPS):
        src = [GROUPS * GX + g, GROUPS * GX + GROUPS + g] + [g * GX + j for j in range(GX)]
        for j, t in enumerate(src):
            w[:, g * GT + j, :] = cw[:, :, t]
            b[:, g * GT + j] = cb[:, t]
    put("cw", w)
    put("cb", b)
    put("dsk", columns(np.repeat(m_d[0], HD)))
    put("ng", columns(m_norm_g[0]))
    fw = columns(f_conv_w).reshape(P, 2, FTAPS, 2, FT)
    put("fw", fw.transpose(0, 1, 4, 3, 2))
    put("fb", columns(f_conv_b).reshape(P, 2, 2, FT).transpose(0, 1, 3, 2))
    put("lng", columns(ln_g))
    put("lnb", columns(ln_b))
    put("kvg", columns(kv_norm_g))
    put("qg", columns(q_norm_g[0]))
    out[0, CC["neg"][0]:CC["neg"][1]] = -1e30
    out[0, CC["one"][0]:CC["one"][1]] = 1.0
    return out


def rotary_tables():
    half = ROPE // 2
    inv = np.float32(10000.0) ** (-np.arange(half, dtype=np.float32) * np.float32(2.0) / np.float32(ROPE))
    ang = (inv[:, None] * np.arange(T, dtype=np.float32)[None, :]).astype(np.float64)
    cos = np.concatenate([np.cos(ang)] * 2, 0)
    sin = np.concatenate([-np.sin(ang), np.sin(ang)], 0)
    q = np.concatenate([np.ones((NOPE, T)), cos, sin], 0) * SC
    return np.stack([q, np.concatenate([cos] * 4, 0), np.concatenate([sin] * 4, 0)], 1).astype(np.float32)


STOP_AT = None


def kernel(x, meta_tokens, m_w_in, m_conv_w, m_conv_b, m_dt_bias, m_a_log, m_d, m_norm_g, m_w_out,
           kv_w_down, kv_norm_g, kv_w_up, q_w_down, q_norm_g, q_w_up, o_w, f_w_in, f_conv_w, f_conv_b,
           f_w_out, ln_g, ln_b):
    import concourse.bacc as bacc
    from concourse.bass_utils import run_bass_kernel_spmd

    a = {k: np.asarray(v) for k, v in locals().items() if isinstance(v, np.ndarray) or hasattr(v, "shape")}
    (x, meta_tokens, m_w_in, m_conv_w, m_conv_b, m_dt_bias, m_a_log, m_d, m_norm_g, m_w_out, kv_w_down,
     kv_norm_g, kv_w_up, q_w_down, q_norm_g, q_w_up, o_w, f_w_in, f_conv_w, f_conv_b, f_w_out, ln_g,
     ln_b) = a.values()
    tokens = np.concatenate([meta_tokens, x[0]], 0)
    arrays = {
        "wstream": weight_stream(m_w_in, m_w_out, kv_w_down, kv_w_up, q_w_down, q_w_up, o_w, f_w_in, f_w_out),
        "xT": np.ascontiguousarray(tokens.reshape(T, KT, P).transpose(2, 1, 0)),
        "consts": constants(m_w_in, m_conv_w, m_conv_b, m_dt_bias, m_a_log, m_d, m_norm_g, kv_norm_g,
                            q_norm_g, f_conv_w, f_conv_b, ln_g, ln_b),
        "tabs": rotary_tables(),
    }
    nc = bacc.Bacc("TRN2", target_bir_lowering=False, num_devices=1)
    aps = [nc.dram_tensor(n, v.shape, F32, kind="ExternalInput").ap() for n, v in arrays.items()]
    out = nc.dram_tensor("outT", (P, KT, SEQ), F32, kind="ExternalOutput").ap()
    build(nc, *aps, out, STOP_AT)
    got = run_bass_kernel_spmd(nc, [arrays], core_ids=[0]).results[0]["outT"]
    return np.ascontiguousarray(got.transpose(2, 1, 0).reshape(1, SEQ, D))
```
